# Optimizing a Trainium2 kernel written in Bass

```python
import math
import jax
import jax.numpy as jnp
from jax import lax
import numpy as np

D_MODEL = 2048
BATCH = 1
SEQ = 256
DEPTH = 1

GDN_HEADS = 8
GDN_DK = 128
GDN_DV = 128
ML_HEADS = 4
ML_DQK = 128
ML_DV = 256
GDN_QK_W = GDN_HEADS * GDN_DK
GDN_V_W = GDN_HEADS * GDN_DV
ML_QK_W = ML_HEADS * ML_DQK
ML_V_W = ML_HEADS * ML_DV
D_MIX = GDN_V_W + ML_V_W
D_FF = 5632
CONV_WIDTH = 4
CHUNK = 64
NORM_EPS = 1e-6
GATE_SOFTCAP = 15.0
PART_SIZES = (GDN_QK_W, GDN_QK_W, GDN_V_W, GDN_V_W, GDN_HEADS, GDN_HEADS,
              ML_QK_W, ML_QK_W, ML_V_W, ML_V_W, ML_HEADS, ML_HEADS)
D_IN_PROJ = sum(PART_SIZES)
SPLIT_IDX = tuple(int(s) for s in np.cumsum(PART_SIZES)[:-1])

kernel_name = 'hybrid_gdn_mlstm_macaron_layer'

def rms_norm(x, w):
    xf = x.astype(jnp.float32)
    y = xf * lax.rsqrt(jnp.mean(xf * xf, axis=-1, keepdims=True) + NORM_EPS)
    return (y * w.astype(jnp.float32)).astype(x.dtype)

def swiglu_ffn(x, w_gate, w_up, w_down):
    return (jax.nn.silu(x @ w_gate) * (x @ w_up)) @ w_down

def l2_normalize(x):
    return x * lax.rsqrt(jnp.sum(x * x, axis=-1, keepdims=True) + NORM_EPS)

def soft_cap(x):
    return GATE_SOFTCAP * jnp.tanh(x / GATE_SOFTCAP)

def causal_depthwise_conv(x, w):
    return lax.conv_general_dilated(
        x, w[:, None, :], window_strides=(1,), padding=[(CONV_WIDTH - 1, 0)],
        dimension_numbers=('NWC', 'WIO', 'NWC'), feature_group_count=x.shape[-1])

def to_chunks(x):
    b, t = x.shape[0], x.shape[1]
    x = x.reshape((b, t // CHUNK, CHUNK) + x.shape[2:])
    return jnp.moveaxis(x, 3, 1)

def from_chunks(o):
    nc, b, h, c, d = o.shape
    return o.transpose(1, 0, 3, 2, 4).reshape(b, nc * c, h, d)

def chunk_masks():
    idx = jnp.arange(CHUNK)
    return idx[:, None] >= idx[None, :], idx[:, None] > idx[None, :]

def gated_delta_rule(q, k, v, g, beta):
    causal, strict = chunk_masks()
    gc = jnp.cumsum(g, axis=-1)
    decay = jnp.exp(jnp.where(causal, gc[..., :, None] - gc[..., None, :], -jnp.inf))
    kb = k * beta[..., None]
    m = jnp.where(strict, jnp.einsum('bhnid,bhnjd->bhnij', kb, k) * decay, 0.0)
    eye = jnp.eye(CHUNK, dtype=q.dtype)
    t_inv = lax.linalg.triangular_solve(eye + m, jnp.broadcast_to(eye, m.shape),
                                        left_side=True, lower=True, unit_diagonal=True)
    u = jnp.einsum('bhnij,bhnje->bhnie', t_inv, v * beta[..., None])
    w = jnp.einsum('bhnij,bhnjd->bhnid', t_inv, kb * jnp.exp(gc)[..., None])
    attn = jnp.einsum('bhnid,bhnjd->bhnij', q, k) * decay
    q_dec = q * jnp.exp(gc)[..., None]
    k_dec = k * jnp.exp(gc[..., -1:] - gc)[..., None]
    g_end = jnp.exp(gc[..., -1])
    xs = tuple(jnp.moveaxis(a, 2, 0) for a in (q_dec, w, u, attn, k_dec, g_end))

    def step(state, inp):
        q_c, w_c, u_c, a_c, k_c, ge = inp
        v_new = u_c - jnp.einsum('bhcd,bhde->bhce', w_c, state)
        o_c = jnp.einsum('bhcd,bhde->bhce', q_c, state) + jnp.einsum('bhij,bhje->bhie', a_c, v_new)
        state = ge[..., None, None] * state + jnp.einsum('bhcd,bhce->bhde', k_c, v_new)
        return state, o_c

    s0 = jnp.zeros((q.shape[0], q.shape[1], q.shape[-1], v.shape[-1]), q.dtype)
    _, o = lax.scan(step, s0, xs)
    return o

def mlstm_chunkwise(q, k, v, i_pre, log_f):
    causal, _ = chunk_masks()
    b = jnp.cumsum(log_f, axis=-1)
    dmat = jnp.where(causal, b[..., :, None] - b[..., None, :] + i_pre[..., None, :], -jnp.inf)
    m_intra = jnp.max(dmat, axis=-1)
    qk = jnp.einsum('bhnid,bhnjd->bhnij', q, k)
    w_log = dmat[..., -1, :]
    b_end = b[..., -1]
    xs = tuple(jnp.moveaxis(a, 2, 0) for a in (q, k, v, b, dmat, m_intra, qk, w_log, b_end))

    def step(carry, inp):
        c_st, n_st, m_st = carry
        q_c, k_c, v_c, b_c, d_c, mi_c, qk_c, wl_c, be_c = inp
        inter_log = b_c + m_st[..., None]
        m_t = jnp.maximum(inter_log, mi_c)
        inter = jnp.exp(inter_log - m_t)
        p = jnp.exp(d_c - m_t[..., None]) * qk_c
        num = inter[..., None] * jnp.einsum('bhcd,bhde->bhce', q_c, c_st) + jnp.einsum('bhij,bhje->bhie', p, v_c)
        den = inter * jnp.einsum('bhcd,bhd->bhc', q_c, n_st) + jnp.sum(p, axis=-1)
        h = num / jnp.maximum(jnp.abs(den), jnp.exp(-m_t))[..., None]
        m_new = m_t[..., -1]
        carry_decay = jnp.exp(be_c + m_st - m_new)
        kw = k_c * jnp.exp(wl_c - m_new[..., None])[..., None]
        c_new = carry_decay[..., None, None] * c_st + jnp.einsum('bhcd,bhce->bhde', kw, v_c)
        n_new = carry_decay[..., None] * n_st + jnp.sum(kw, axis=-2)
        return (c_new, n_new, m_new), h

    bsz, heads = q.shape[0], q.shape[1]
    init = (jnp.zeros((bsz, heads, q.shape[-1], v.shape[-1]), q.dtype),
            jnp.zeros((bsz, heads, q.shape[-1]), q.dtype),
            jnp.zeros((bsz, heads), q.dtype))
    _, h = lax.scan(step, init, xs)
    return h

def hybrid_mixer(h, w_in, conv_w, gdn_a_log, gdn_dt_bias, gdn_norm_w, ml_i_bias, ml_f_bias, w_out):
    bsz, t, _ = h.shape
    f32 = jnp.float32
    proj = (h @ w_in).astype(f32)
    gq, gk, gv, gz, ga, gb, mq, mk, mv, mo, mi, mf = jnp.split(proj, SPLIT_IDX, axis=-1)

    qkv = jax.nn.silu(causal_depthwise_conv(jnp.concatenate([gq, gk, gv], axis=-1), conv_w.astype(f32)))
    gq, gk, gv = jnp.split(qkv, [GDN_QK_W, 2 * GDN_QK_W], axis=-1)
    q = l2_normalize(gq.reshape(bsz, t, GDN_HEADS, GDN_DK)) * (GDN_DK ** -0.5)
    k = l2_normalize(gk.reshape(bsz, t, GDN_HEADS, GDN_DK))
    v = gv.reshape(bsz, t, GDN_HEADS, GDN_DV)
    g = -jnp.exp(gdn_a_log.astype(f32)) * jax.nn.softplus(ga + gdn_dt_bias.astype(f32))
    beta = jax.nn.sigmoid(gb)
    o = from_chunks(gated_delta_rule(to_chunks(q), to_chunks(k), to_chunks(v), to_chunks(g), to_chunks(beta)))
    o = o * lax.rsqrt(jnp.mean(o * o, axis=-1, keepdims=True) + NORM_EPS) * gdn_norm_w.astype(f32)
    o = o * jax.nn.silu(gz.reshape(bsz, t, GDN_HEADS, GDN_DV))
    y_gdn = o.reshape(bsz, t, GDN_V_W)

    q = mq.reshape(bsz, t, ML_HEADS, ML_DQK) * (ML_DQK ** -0.5)
    k = mk.reshape(bsz, t, ML_HEADS, ML_DQK)
    v = mv.reshape(bsz, t, ML_HEADS, ML_DV)
    i_pre = soft_cap(mi + ml_i_bias.astype(f32))
    log_f = jax.nn.log_sigmoid(soft_cap(mf + ml_f_bias.astype(f32)))
    hm = from_chunks(mlstm_chunkwise(to_chunks(q), to_chunks(k), to_chunks(v), to_chunks(i_pre), to_chunks(log_f)))
    y_ml = jax.nn.sigmoid(mo) * hm.reshape(bsz, t, ML_V_W)

    y = jnp.concatenate([y_gdn, y_ml], axis=-1).astype(h.dtype)
    return y @ w_out

def setup_inputs(seed: int = 0) -> dict:
    key = jax.random.key(seed)
    ks = jax.random.split(key, 24)
    f32 = jnp.float32

    def normal(k, shape, scale):
        return jax.random.normal(k, shape, f32) * scale

    def gain(k, shape):
        return 1.0 + 0.02 * jax.random.normal(k, shape, f32)

    x = normal(ks[0], (BATCH, SEQ, D_MODEL), 1.0)
    ffn1_norm_w = gain(ks[1], (DEPTH, D_MODEL))
    ffn1_w_gate = normal(ks[2], (DEPTH, D_MODEL, D_FF), D_MODEL ** -0.5)
    ffn1_w_up = normal(ks[3], (DEPTH, D_MODEL, D_FF), D_MODEL ** -0.5)
    ffn1_w_down = normal(ks[4], (DEPTH, D_FF, D_MODEL), D_FF ** -0.5)
    mix_norm_w = gain(ks[5], (DEPTH, D_MODEL))
    w_in = normal(ks[6], (DEPTH, D_MODEL, D_IN_PROJ), D_MODEL ** -0.5)
    conv_w = normal(ks[7], (DEPTH, CONV_WIDTH, 2 * GDN_QK_W + GDN_V_W), CONV_WIDTH ** -0.5)
    gdn_a_log = jnp.log(jax.random.uniform(ks[8], (DEPTH, GDN_HEADS), f32, 1.0, 16.0))
    dt = jnp.exp(jax.random.uniform(ks[9], (DEPTH, GDN_HEADS), f32, math.log(1e-3), math.log(1e-1)))
    gdn_dt_bias = dt + jnp.log(-jnp.expm1(-dt))
    gdn_norm_w = gain(ks[10], (DEPTH, GDN_DV))
    ml_i_bias = normal(ks[11], (DEPTH, ML_HEADS), 0.1)
    ml_f_bias = jnp.linspace(3.0, 6.0, ML_HEADS, dtype=f32)[None, :] + normal(ks[12], (DEPTH, ML_HEADS), 0.1)
    w_out = normal(ks[13], (DEPTH, D_MIX, D_MODEL), D_MIX ** -0.5)
    ffn2_norm_w = gain(ks[14], (DEPTH, D_MODEL))
    ffn2_w_gate = normal(ks[15], (DEPTH, D_MODEL, D_FF), D_MODEL ** -0.5)
    ffn2_w_up = normal(ks[16], (DEPTH, D_MODEL, D_FF), D_MODEL ** -0.5)
    ffn2_w_down = normal(ks[17], (DEPTH, D_FF, D_MODEL), D_FF ** -0.5)
    final_norm_w = gain(ks[18], (D_MODEL,))
    return {'x': x, 'ffn1_norm_w': ffn1_norm_w, 'ffn1_w_gate': ffn1_w_gate, 'ffn1_w_up': ffn1_w_up,
            'ffn1_w_down': ffn1_w_down, 'mix_norm_w': mix_norm_w, 'w_in': w_in, 'conv_w': conv_w,
            'gdn_a_log': gdn_a_log, 'gdn_dt_bias': gdn_dt_bias, 'gdn_norm_w': gdn_norm_w,
            'ml_i_bias': ml_i_bias, 'ml_f_bias': ml_f_bias, 'w_out': w_out, 'ffn2_norm_w': ffn2_norm_w,
            'ffn2_w_gate': ffn2_w_gate, 'ffn2_w_up': ffn2_w_up, 'ffn2_w_down': ffn2_w_down,
            'final_norm_w': final_norm_w}

def reference(x, ffn1_norm_w, ffn1_w_gate, ffn1_w_up, ffn1_w_down, mix_norm_w, w_in, conv_w,
              gdn_a_log, gdn_dt_bias, gdn_norm_w, ml_i_bias, ml_f_bias, w_out, ffn2_norm_w,
              ffn2_w_gate, ffn2_w_up, ffn2_w_down, final_norm_w):
    h = x
    for l in range(DEPTH):
        h = h + 0.5 * swiglu_ffn(rms_norm(h, ffn1_norm_w[l]), ffn1_w_gate[l], ffn1_w_up[l], ffn1_w_down[l])
        h = h + hybrid_mixer(rms_norm(h, mix_norm_w[l]), w_in[l], conv_w[l], gdn_a_log[l], gdn_dt_bias[l],
                             gdn_norm_w[l], ml_i_bias[l], ml_f_bias[l], w_out[l])
        h = h + 0.5 * swiglu_ffn(rms_norm(h, ffn2_norm_w[l]), ffn2_w_gate[l], ffn2_w_up[l], ffn2_w_down[l])
    return rms_norm(h, final_norm_w)


_drawn_inputs = setup_inputs


def setup_inputs(seed=0):
    import zlib

    import numpy as np

    out = dict(_drawn_inputs(seed))
    spreads = {}
    factors = {'gdn_norm_w': 8.0, 'ml_i_bias': 4.165, 'ffn2_norm_w': 8.0, 'final_norm_w': 2.838}
    for name, (base, spread) in spreads.items():
        noise = np.random.default_rng([zlib.crc32(name.encode()), seed]).standard_normal(out[name].shape)
        drawn = base * np.exp(spread * noise) if base else spread * noise
        out[name] = jnp.asarray(drawn.astype(out[name].dtype))
    for name, factor in factors.items():
        out[name] = (out[name] * factor).astype(out[name].dtype)
    return out
```

```python
from contextlib import ExitStack

import numpy as np

import concourse.bass as bass
from concourse import mybir

F32 = mybir.dt.float32
F32R = mybir.dt.float32r
ACTF = mybir.ActivationFunctionType
ALU = mybir.AluOpType

P = 128
T = 256
D = 2048
DT_ = D // P
F = 5632
UK = 4
UN = 256
BLK_A, BLK_B = 12, 10
NJD = D // UN
HG, HM = 8, 4
NQKV = 3 * HG
NREST = HG + 2 * HM + 2 * 2 * HM
NG = 2 * HG + 2 * HM
CW = 4
C = 128
NCH = T // C
EPS = 1e-6
CAP = 15.0
STAGES = 4
SLOTS = 4
LEVELS = [1, 2, 4, 8, 16, 32, 64]

U_FFN_BLOCK = 2 * DT_ // UK
U_IN = (NQKV + NREST) // 2 * (DT_ // UK)
U_OUT = NJD * DT_ // UK
U_DOWN_A, U_DOWN_B = 2 * BLK_A // UK, 2 * BLK_B // UK
U_FFN = (BLK_A + BLK_B) * U_FFN_BLOCK + NJD * (U_DOWN_A + U_DOWN_B)
UNITS = 2 * U_FFN + U_IN + U_OUT

S_NORM = 0
S_CONV = S_NORM + 4 * DT_
S_GNW = S_CONV + NQKV * CW
S_BIAS = S_GNW + 1
S_ALOG = S_BIAS + NG
S_N = S_ALOG + HG
K_ID, K_TRI, K_LOW, K_LEV = 0, P, 2 * P, 3 * P
K_N = K_LEV + len(LEVELS) * P


def constants():
    r, c = np.arange(P)[:, None], np.arange(P)[None, :]
    parts = [r == c, c >= r, c < r]
    for b in LEVELS:
        parts.append((r // (2 * b) == c // (2 * b)) & (r // b % 2 == 1) & (c // b % 2 == 0))
    return np.concatenate(parts, axis=1).astype(np.float32)


def build(nc, stream, x, wg, small, consts, out):
    with ExitStack() as ctx:
        base = (nc.sbuf_base + 63) // 64 * 64
        cursor = [base]
        def sb(name, shape, dt, at=None):
            size = int(np.prod(shape[1:])) * 4
            size = (size + 31) // 32 * 32
            if at is None:
                at = cursor[0]
                cursor[0] += size
                assert cursor[0] <= nc.sbuf_usable_end, name
            return nc.alloc_sbuf_tensor_at(name, shape, dt, offset=at), at + size

        def sem(name):
            return ctx.enter_context(nc.semaphore(name))

        st, _ = sb("stage", [P, STAGES, UK, UN], F32)
        whi, _ = sb("w_hi", [P, SLOTS, UK, UN], F32R)
        wlo, _ = sb("w_lo", [P, SLOTS, UK, UN], F32R)
        xs, _ = sb("x_split", [P, DT_, 2 * T], F32R)
        res, _ = sb("residual", [P, DT_, T], F32)
        hs_at = cursor[0]
        hs, hs_end = sb("h_split", [P, 2 * BLK_A, 2 * T], F32R)
        qkv, _ = sb("qkv", [P, NQKV, T], F32)
        kc, _ = sb("constants", [P, K_N], F32)
        sm, _ = sb("small", [P, S_N], F32)
        rstd, _ = sb("rstd", [P, T], F32)
        ssq, _ = sb("sum_sq", [P, 2, T], F32)
        ones_t, _ = sb("ones", [P, P], F32)
        ones = ones_t[:]
        eps, _ = sb("eps", [P, 1], F32)
        tmp, _ = sb("low_part", [P, 2, 2, T], F32)
        both = cursor[0]
        gsum, at = sb("gate_sum", [P, 2, T], F32)
        sg, at = sb("gate_silu", [P, 2, T], F32)
        usum, at = sb("up_sum", [P, 2, T], F32)
        hp, at = sb("h_full", [P, 2, T], F32)
        sq, at = sb("squares", [P, 2, T], F32)
        nt, at = sb("normed", [P, 2, 4, T], F32)
        ffn_end = at
        rest, at = sb("rest", [P, NREST, T], F32, at=hs_at)
        tail = at
        X, at = sb("inv_x", [P, NCH, 4, C], F32, at=at)
        Y, at = sb("inv_y", [P, NCH, 4, C], F32, at=at)
        Z, at = sb("inv_z", [P, NCH, 4, C], F32, at=at)
        L, at = sb("inv_l", [P, NCH, 4, C], F32, at=at)
        assert at <= hs_end
        wgf, _ = sb("wgate", [P, DT_, NG], F32, at=at - 4 * NCH * C * 4)
        raw, at = sb("conv_in", [P, 2, CW - 1 + T], F32, at=tail)
        cv, at = sb("conv_half", [P, 2, T], F32, at=at)
        cth, at = sb("conv_tanh", [P, 2, T], F32, at=at)
        M, at = sb("coupling", [P, NCH, 4, C], F32, at=both)
        DTr, at = sb("decay_t", [P, NCH, 4, C], F32, at=at)
        R, at = sb("rhs_v", [P, NCH, 4, C], F32, at=at)
        V1, at = sb("v_tok1", [P, 4, C], F32, at=at)
        KD, at = sb("k_dec", [P, 4, C], F32, at=at)
        ER, at = sb("exp_gc_row1", [P, 4, C], F32, at=at)
        gcrow, at = sb("gc_rows", [HG, T], F32, at=at)
        mrow, at = sb("m_rows", [HM, 2, T], F32, at=at)
        gt, at = sb("gates_tok", [P, NCH, NG], F32, at=at)
        th, at = sb("tanh", [P, NCH, 2 * HM], F32, at=at)
        beta, at = sb("beta", [P, NCH, HG], F32, at=at)
        ipre, at = sb("i_pre", [P, NCH, HM], F32, at=at)
        spi, at = sb("softplus_in", [P, NCH, HG + HM], F32, at=at)
        spa, at = sb("softplus_abs", [P, NCH, HG + HM], F32, at=at)
        gl, at = sb("g_and_neg_logf", [P, NCH, HG + HM], F32, at=at)
        rate, at = sb("decay_rate", [P, HG], F32, at=at)
        cum, at = sb("cum_cols", [P, NCH, HG + HM], F32, at=at)
        egn, at = sb("neg_exp_gc", [P, NCH, HG], F32, at=at)
        acol, at = sb("a_cols", [P, NCH, HM], F32, at=at)
        dcol, at = sb("decay_to_end", [P, 4], F32, at=at)
        cursor[0] = max(ffn_end, at)
        glo, at = sb("gates_low", [NG, T], F32, at=both)
        g24, at = sb("gates_rows", [NG, T], F32, at=at)
        srow, at = sb("s_rows", [HM, T], F32, at=at)
        crow, at = sb("cummax_rows", [HM, 2, C + T], F32, at=at)
        wgh, _ = sb("wgate_hi", [P, DT_, NG], F32R)
        wgl, _ = sb("wgate_lo", [P, DT_, NG], F32R)

        pg = ctx.enter_context(nc.psum_tensor("gemm_banks", [P, 2, 2, 512], F32))
        pp = ctx.enter_context(nc.psum_tensor("side_banks", [P, 4, 512], F32))

        ident = kc[:, K_ID:K_ID + P]
        tri, low = kc[:, K_TRI:K_TRI + P], kc[:, K_LOW:K_LOW + P]

        def level(n):
            return kc[:, K_LEV + n * P:K_LEV + (n + 1) * P]

        def row_to_all(n, h):
            return kc[0:n, K_ID + h:K_ID + h + 1].to_broadcast([n, P])

        def over(ap, n):
            return ap.rearrange("p (a m) -> p a m", a=1).to_broadcast([ap.shape[0], n, ap.shape[1]])

        small_in = sem("small_landed")
        consts_in = sem("constants_landed")
        wg_in = sem("wgate_landed")
        x_in = [sem(f"x_landed_{q}") for q in range(4)]
        staged = [sem(f"unit_landed_{s}") for s in range(STAGES)]
        hi_ready = sem("hi_ready")
        split = sem("unit_split")
        unit_done = sem("unit_done")
        bank_free = sem("bank_free")
        lo_copied = sem("lo_copied")
        gate_tanh = sem("gate_tanh")
        gate_act = sem("gate_activated")
        h_ready = sem("h_ready")
        h_hi = sem("h_hi_ready")
        h_split = sem("h_split_ready")
        res_done = sem("residual_updated")
        sq_done = sem("squares_ready")
        ssq_part = sem("sum_sq_added")
        x_sq = sem("x_squares_ready")
        x_sq_mm = sem("x_squares_summed")
        ssq_mm = sem("sum_sq_total")
        ln_done = sem("ln_sum_sq")
        rstd_done = sem("rstd_ready")
        t_ready = sem("normed_ready")
        x_hi = sem("x_hi_ready")
        x_ready = sem("x_split_ready")
        fills = sem("constants_filled")
        wg_hi = sem("wgate_hi_ready")
        wg_split = sem("wgate_split")
        tap0 = sem("conv_tap0")
        conv_step = sem("conv_step")
        conv_tanh = sem("conv_tanh")
        qkv_done = sem("qkv_done")
        out_done = [sem(f"out_landed_{b}") for b in range(2)]

        w_cols = lambda n, k: sm[:, S_NORM + n * DT_ + k:S_NORM + n * DT_ + k + 1]

        plan, u, j = {}, 0, 0
        for name, jobs, per, n_units, rounds in [
            ("ffn1_up_a", 2 * BLK_A, 2, DT_ // UK, BLK_A), ("ffn1_down_a", NJD, 2, U_DOWN_A, NJD // 2),
            ("ffn1_up_b", 2 * BLK_B, 2, DT_ // UK, BLK_B), ("ffn1_down_b", NJD, 4, U_DOWN_B, NJD // 4),
            ("in_qkv", NQKV // 2, 2, DT_ // UK, NQKV // 4), ("in_rest", NREST // 2, 2, DT_ // UK, NREST // 4),
            ("out", NJD, 2, DT_ // UK, NJD // 2),
            ("ffn2_up_a", 2 * BLK_A, 2, DT_ // UK, BLK_A), ("ffn2_down_a", NJD, 2, U_DOWN_A, NJD // 2),
            ("ffn2_up_b", 2 * BLK_B, 2, DT_ // UK, BLK_B), ("ffn2_down_b", NJD, 4, U_DOWN_B, NJD // 4),
        ]:
            assert per * rounds == jobs and per * n_units % SLOTS == 0 and u % SLOTS == 0 and j % 2 == 0
            plan[name] = (u, j, per, n_units, rounds)
            u, j = u + jobs * n_units, j + jobs
        assert u == UNITS

        def rounds_of(eng, name):
            rounds = plan[name][4]
            if name in ("ffn2_down_b", "in_rest"):
                yield from range(rounds)
            else:
                with eng.Fori(0, rounds) as i:
                    yield i

        gates_mm, gates_lo, gates_sum, gates_t = sem("gates_mm"), sem("gates_low"), sem("gates_sum"), sem("gates_turned")
        gt_ready, gt_act, sp_in, sp_ln = sem("gates_biased"), sem("gates_tanh_exp"), sem("softplus_in"), sem("softplus_ln")
        gl_ready, cum_mm, rows_ready, gc_ready = sem("g_ready"), sem("cum_sums_mm"), sem("rows_ready"), sem("gc_cols_ready")
        mrows_ready = sem("m_rows_ready")
        eg_done = sem("exp_gc_done")
        l2_sq, l2_mm, l2_ln, l2_std, l2_done = sem("l2_squares"), sem("l2_sums"), sem("l2_ln"), sem("l2_rstd"), sem("l2_done")
        rb_mm, rb_pre, er_done, dec_exp = sem("gc_on_all_mm"), sem("gc_differences"), sem("exp_gc_row"), sem("decay_exp")
        qk_mm, at_done, kk_mm, m_done = sem("qk_mm"), sem("attn_done"), sem("kk_mm"), sem("coupling_done")
        vt_mm, v_done, kt_mm, kd_done = sem("v_turned"), sem("v_scaled"), sem("k_turned"), sem("k_dec_done")
        x1_ready, y1_mm, y1_done = sem("x1_ready"), sem("x1_turned"), sem("y1_copied")
        y_done, x_done = sem("y_updated"), sem("x_updated")
        l_ready, z_mm, z_done = sem("l_masked"), sem("z_mm"), sem("z_copied")
        yz_mm, xz_mm = sem("yz_mm"), sem("xz_mm")
        vn_mm, vn_done = sem("v_new_mm"), sem("v_new_copied")
        s1_mm, s1_done, ks_mm, r1_done, qd_done = sem("state_mm"), sem("state_copied"), sem("k_state_mm"), sem("r1_done"), sem("q_dec_done")
        o_mm, o_done = sem("o_mm"), sem("o_copied")
        gz_tanh, gz_done = sem("gz_tanh"), sem("gz_gate_done")
        on_sq, on_mm, on_ln, on_std, on_pre, on_hi = (sem("o_squares"), sem("o_sums"), sem("o_ln"), sem("o_rstd"),
                                                      sem("o_gated"), sem("y_hi"))
        y_split = sem("y_split_ready")
        mb_mm, me_pre, me_exp, mx_exp = sem("m_on_all_mm"), sem("m_differences"), sem("m_weights_exp"), sem("m_floor_exp")
        mqk_mm, p_done, mv_mm, mvt_done = sem("m_qk_mm"), sem("p_done"), sem("m_v_turned"), sem("m_v_copied")
        num_mm, mh_done = sem("m_num_mm"), sem("m_h_done")
        mo_tanh, my_pre, my_hi = sem("mo_tanh"), sem("m_gated"), sem("m_y_hi")
        dve_step = sem("dve_step")
        act_step = sem("act_step")

        NL = len(LEVELS) - 1
        pairs = HG // 2
        q_at, k_at, v_at = 0, HG, 2 * HG
        gz_at, mq_at, mk_at, mv_at, mo_at = 0, HG, HG + HM, HG + 2 * HM, HG + 4 * HM
        rest_job0 = plan["in_rest"][1]
        mv_jobs = rest_job0 + mo_at // 2

        def half(buf, n):
            return buf[:, n].rearrange("p h c -> p (h c)")

        def slot(buf, n):
            return half(buf, n).rearrange("p (a t) -> p a t", a=2)

        def tiles(buf):
            return buf[:].rearrange("p n h c -> p (n h) c")

        def chunk(buf, tile, c):
            return buf[:, tile, c * C:(c + 1) * C]

        def bank(b, h):
            return pp[:, b, h * C:(h + 1) * C]

        def gz_gate(p):
            at = (q_at if p < 2 else k_at) + p % 2 * 2
            return qkv[:, at:at + 2, :]

        sums = [(buf, n) for buf in (X, Y, Z, L) for n in range(2)]
        mE = [half(DTr, n)[:, 0:3 * C] for n in range(2)]
        mP = [half(M, n)[:, 0:3 * C] for n in range(2)]
        mV = [Z[:, n] for n in range(2)]
        mX = half(L, 0).rearrange("p (a t) -> p a t", a=2)
        mDn = half(L, 1).rearrange("p (a t) -> p a t", a=2)
        mY = [slot(R, n) for n in range(2)]

        def mixer_pe(pe):
            pe.wait_ge(wg_split, 1)
            for k in range(DT_):
                pe.matmul(pp[0:NG, 0, :], wgh[:, k, :], xs[:, k, :], start=k == 0, stop=False, skip_group_check=True)
                mm = pe.matmul(pp[0:NG, 0, 0:T], wgl[:, k, :], xs[:, k, 0:T], start=False, stop=k == DT_ - 1,
                               skip_group_check=True)
            mm.then_inc(gates_mm, 1)
            pe.wait_ge(consts_in, 16)
            yield
            for g in range(HG):
                if g == 0:
                    pe.wait_ge(gates_sum, 1)
                    for c in range(NCH):
                        mm = pe.transpose(pp[:, 1, c * 32:c * 32 + NG], g24[:, c * C:(c + 1) * C], ident[0:NG, 0:NG])
                    mm.then_inc(gates_t, 1)
                pe.wait_ge(l2_sq, g + 1)
                if g >= 2:
                    pe.wait_ge(l2_ln, g - 1)
                pe.matmul(pp[:, 2 + g % 2, :], ones, half(*sums[g]), start=True, stop=True).then_inc(l2_mm, 1)
                if g % 2:
                    yield
            pe.wait_ge(gl_ready, 1)
            n = HG + HM
            for c in range(NCH):
                pe.matmul(pp[:, 0, c * n:(c + 1) * n], tri, gl[:, c, :], start=True, stop=True, skip_group_check=True)
            pe.matmul(pp[:, 0, n + HG:2 * n], ones, gl[:, 0, HG:n], start=False, stop=True, skip_group_check=True)
            for c in range(NCH):
                pe.matmul(pp[0:HG, 1, c * C:(c + 1) * C], gl[:, c, 0:HG], tri, start=True, stop=True, skip_group_check=True)
            for c in range(NCH):
                pe.matmul(pp[0:HM, 0, T + c * C:T + (c + 1) * C], ipre[:, c, :], ident, start=True, stop=True,
                          skip_group_check=True)
            for c in range(NCH):
                mm = pe.matmul(pp[0:HM, 1, T + c * C:T + (c + 1) * C], gl[:, c, HG:n], tri, start=True, stop=True,
                               skip_group_check=True)
            mm = pe.matmul(pp[0:HM, 1, T + C:2 * T], gl[:, 0, HG:n], ones, start=False, stop=True, skip_group_check=True)
            mm.then_inc(cum_mm, 1)
            yield
            yield
            pe.wait_ge(rows_ready, 1)
            for grp in range(2):
                yield from group_pe(pe, grp)
            for p in range(pairs):
                pe.wait_ge(on_sq, p + 1)
                if p >= 2:
                    pe.wait_ge(on_ln, p - 1)
                pe.matmul(pp[:, 2 + p % 2, :], ones, half(*sums[p]), start=True, stop=True).then_inc(on_mm, 1)
                if p % 2:
                    yield
            pe.wait_ge(on_ln, pairs)
            pe.wait_ge(mrows_ready, 1)
            pe.wait_ge(bank_free, 2 + mv_jobs)
            for m in range(HM):
                if m:
                    pe.wait_ge(mvt_done, m)
                    pe.wait_ge(me_pre, m)
                pe.matmul(pp[:, 0, :], row_to_all(HM, m), mrow[:].rearrange("h a t -> h (a t)"),
                          start=True, stop=True).then_inc(mb_mm, 1)
                for c in range(NCH):
                    for e in range(2):
                        mm = pe.transpose(pp[:, 2, (2 * c + e) * C:(2 * c + e + 1) * C],
                                          chunk(rest, mv_at + 2 * m + e, c), ident)
                mm.then_inc(mv_mm, 1)
                if m:
                    pe.wait_ge(mh_done, m)
                q, k = rest[:, mq_at + m], rest[:, mk_at + m]
                pe.matmul(pp[:, 1, 0:T], k[:, 0:C], q, start=True, stop=True, skip_group_check=True)
                pe.matmul(pp[:, 1, T:T + C], k[:, C:T], q[:, C:T], start=True, stop=True,
                          skip_group_check=True).then_inc(mqk_mm, 1)
                yield
                pe.wait_ge(p_done, m + 1)
                pe.wait_ge(mvt_done, m + 1)
                v, w = mV[m % 2], mP[m % 2]
                for e in range(2):
                    pe.matmul(pp[:, 3, e * T:(e + 1) * T], v[:, e], w[:, 0:T], start=True, stop=False, skip_group_check=True)
                    pe.matmul(pp[:, 3, e * T + C:(e + 1) * T], v[:, 2 + e], w[:, T:3 * C], start=False, stop=True,
                              skip_group_check=True)
                pe.matmul(pp[:, 1, 0:T], ones, w[:, 0:T], start=True, stop=False, skip_group_check=True)
                pe.matmul(pp[:, 1, C:T], ones, w[:, T:3 * C], start=False, stop=True,
                          skip_group_check=True).then_inc(num_mm, 1)
                yield

        def group_pe(pe, grp):
            h0 = 4 * grp
            q = lambda h, c: chunk(qkv, q_at + h0 + h, c)
            k = lambda h, c: chunk(qkv, k_at + h0 + h, c)
            v = lambda h, c: chunk(qkv, v_at + h0 + h, c)
            if grp:
                pe.wait_ge(o_done, 2 * grp)
            for h in range(4):
                mm = pe.matmul(pp[:, h // 2, h % 2 * T:(h % 2 + 1) * T], row_to_all(HG, h0 + h), gcrow[:],
                               start=True, stop=True, skip_group_check=True)
            mm.then_inc(rb_mm, 1)
            pe.wait_ge(l2_done, HG)
            for c in range(NCH):
                for h in range(4):
                    mm = pe.matmul(bank(2 + c, h), k(h, c), q(h, c), start=True, stop=True, skip_group_check=True)
            mm.then_inc(qk_mm, 1)
            yield
            pe.wait_ge(rb_pre, grp + 1)
            pe.wait_ge(er_done, grp + 1)
            for c in range(NCH):
                for h in range(4):
                    mm = pe.matmul(bank(c, h), k(h, c), k(h, c), start=True, stop=True, skip_group_check=True)
            mm.then_inc(kk_mm, 1)
            yield
            pe.wait_ge(at_done, grp + 1)
            for c in range(NCH):
                for h in range(4):
                    mm = pe.transpose(bank(2 + c, h), v(h, c), ident)
            mm.then_inc(vt_mm, 1)
            yield
            pe.wait_ge(m_done, grp + 1)
            for h in range(4):
                mm = pe.transpose(bank(0, h), k(h, 0), ident)
            mm.then_inc(kt_mm, 1)
            yield
            pe.wait_ge(x1_ready, grp + 1)
            pe.wait_ge(kd_done, grp + 1)
            for c in range(NCH):
                for h in range(4):
                    mm = pe.transpose(bank(c, h), X[:, c, h], ident)
            mm.then_inc(y1_mm, 1)
            yield
            for n in range(NL):
                pe.wait_ge(l_ready, grp * NL + n + 1)
                if n == 0:
                    pe.wait_ge(y1_done, grp + 1)
                    pe.wait_ge(v_done, grp + 1)
                else:
                    pe.wait_ge(y_done, grp * NL + n)
                    pe.wait_ge(x_done, grp * (NL - 1) + n)
                for c in range(NCH):
                    for h in range(4):
                        mm = pe.matmul(bank(2 + c, h), L[:, c, h], Y[:, c, h], start=True, stop=True, skip_group_check=True)
                mm.then_inc(z_mm, 1)
                yield
                pe.wait_ge(z_done, grp * NL + n + 1)
                for c in range(NCH):
                    for h in range(4):
                        mm = pe.matmul(bank(c, h), X[:, c, h], Z[:, c, h], start=True, stop=True, skip_group_check=True)
                mm.then_inc(yz_mm, 1)
                if n < NL - 1:
                    for c in range(NCH):
                        for h in range(4):
                            mm = pe.matmul(bank(2 + c, h), Z[:, c, h], X[:, c, h], start=True, stop=True, skip_group_check=True)
                    mm.then_inc(xz_mm, 1)
                yield
            pe.wait_ge(y_done, (grp + 1) * NL)
            for h in range(4):
                mm = pe.matmul(bank(2, h), Y[:, 0, h], R[:, 0, h], start=True, stop=True, skip_group_check=True)
            mm.then_inc(vn_mm, 1)
            yield
            pe.wait_ge(vn_done, 2 * grp + 1)
            for h in range(4):
                mm = pe.matmul(bank(3, h), KD[:, h], Z[:, 0, h], start=True, stop=True, skip_group_check=True)
            mm.then_inc(s1_mm, 1)
            for h in range(4):
                mm = pe.matmul(bank(2, h), Z[:, 0, h], DTr[:, 0, h], start=True, stop=True, skip_group_check=True)
            mm.then_inc(o_mm, 1)
            yield
            pe.wait_ge(s1_done, grp + 1)
            for h in range(4):
                mm = pe.matmul(bank(0, h), k(h, 1), L[:, 0, h], start=True, stop=True, skip_group_check=True)
            mm.then_inc(ks_mm, 1)
            yield
            pe.wait_ge(r1_done, grp + 1)
            for h in range(4):
                mm = pe.matmul(bank(1, h), Y[:, 1, h], R[:, 1, h], start=True, stop=True, skip_group_check=True)
            mm.then_inc(vn_mm, 1)
            yield
            pe.wait_ge(qd_done, grp + 1)
            pe.wait_ge(vn_done, 2 * grp + 2)
            for h in range(4):
                pe.matmul(bank(3, h), L[:, 0, h], L[:, 1, h], start=True, stop=False, skip_group_check=True)
                mm = pe.matmul(bank(3, h), Z[:, 1, h], DTr[:, 1, h], start=False, stop=True, skip_group_check=True)
            mm.then_inc(o_mm, 1)
            yield

        def mixer_act(act):
            act.wait_ge(qkv_done, NQKV // 2)
            for g in range(HG // 2):
                act.activation(slot(*sums[g]), qkv[:, 2 * g:2 * g + 2, :], ACTF.Square).then_inc(l2_sq, 1)
            act.wait_ge(gates_mm, 1)
            act.activation(glo[:], pp[0:NG, 0, T:2 * T], ACTF.Copy).then_inc(gates_lo, 1)
            for g in range(HG // 2, HG):
                act.activation(slot(*sums[g]), qkv[:, 2 * g:2 * g + 2, :], ACTF.Square).then_inc(l2_sq, 1)
            yield
            for g in range(HG):
                if g == 2:
                    act.wait_ge(gt_ready, 1)
                    act.activation(th[:], gt[:, :, 2 * HG:NG], ACTF.Tanh, scale=1.0 / CAP)
                    act.activation(beta[:], gt[:, :, HG:2 * HG], ACTF.Exp, scale=-1.0)
                    act.activation(rate[:], sm[:, S_ALOG:S_ALOG + HG], ACTF.Exp).then_inc(gt_act, 1)
                    act.wait_ge(sp_in, 1)
                    act.activation(spa[:], spa[:], ACTF.Exp).then_inc(act_step, 1)
                    act.wait_ge(act_step, 1)
                    act.activation(spa[:], spa[:], ACTF.Ln, bias=1.0).then_inc(sp_ln, 1)
                act.wait_ge(l2_mm, g + 1)
                act.activation(half(*sums[g]), pp[:, 2 + g % 2, :], ACTF.Ln, bias=eps[:]).then_inc(l2_ln, 1)
                if g % 2:
                    yield
            act.wait_ge(l2_ln, HG)
            for b in range(4):
                act.activation(tiles(sums[2 * b][0]), tiles(sums[2 * b][0]), ACTF.Exp, scale=-0.5).then_inc(l2_std, 1)
            act.wait_ge(gc_ready, 1)
            act.activation(egn[:], cum[:, :, 0:HG], ACTF.Exp).then_inc(eg_done, 1)
            yield
            yield
            for grp in range(2):
                yield from group_act(act, grp)
            act.wait_ge(o_done, 4)
            for p in range(pairs):
                act.activation(slot(*sums[p]), qkv[:, v_at + 2 * p:v_at + 2 * p + 2, :], ACTF.Square).then_inc(on_sq, 1)
            for p in range(pairs):
                act.wait_ge(on_mm, p + 1)
                act.activation(half(*sums[p]), pp[:, 2 + p % 2, :], ACTF.Ln, bias=eps[:], scale=1.0 / P).then_inc(on_ln, 1)
                if p % 2:
                    yield
            act.wait_ge(on_ln, pairs)
            for b in range(2):
                act.activation(tiles(sums[2 * b][0]), tiles(sums[2 * b][0]), ACTF.Exp, scale=-0.5).then_inc(on_std, 1)
            for m in range(HM):
                act.wait_ge(me_pre, m + 1)
                act.activation(mE[m % 2], mE[m % 2], ACTF.Exp, scale=-1.0).then_inc(me_exp, 1)
                act.activation(mX[:, m % 2], pp[:, 0, T:2 * T], ACTF.Exp).then_inc(mx_exp, 1)
                act.wait_ge(mv_mm, m + 1)
                act.activation(mV[m % 2], pp[:, 2, :].rearrange("p (a c) -> p a c", a=4), ACTF.Copy).then_inc(mvt_done, 1)
                yield
                yield

        def group_act(act, grp):
            act.wait_ge(rb_mm, grp + 1)
            for b in range(2):
                ins = act.activation(ER[:, 2 * b:2 * b + 2], pp[:, b, :].rearrange("p (h t) -> p h t", h=2)[:, :, C:T], ACTF.Exp)
            ins.then_inc(er_done, 1)
            yield
            act.wait_ge(rb_pre, grp + 1)
            act.activation(tiles(DTr), tiles(DTr), ACTF.Exp)
            act.activation(tiles(M), tiles(M), ACTF.Exp, scale=-1.0).then_inc(dec_exp, 1)
            if grp:
                for p in range(pairs):
                    ins = act.activation(gz_gate(p), rest[:, gz_at + 2 * p:gz_at + 2 * p + 2], ACTF.Tanh, scale=0.5)
                ins.then_inc(gz_tanh, 1)
            yield
            yield
            yield
            act.wait_ge(y1_mm, grp + 1)
            for c in range(NCH):
                ins = act.activation(half(Y, c), pp[:, c, :], ACTF.Copy)
            ins.then_inc(y1_done, 1)
            yield
            for n in range(NL):
                act.wait_ge(z_mm, grp * NL + n + 1)
                for c in range(NCH):
                    ins = act.activation(half(Z, c), pp[:, 2 + c, :], ACTF.Copy)
                ins.then_inc(z_done, 1)
                yield
                yield
            act.wait_ge(vn_mm, 2 * grp + 1)
            act.activation(half(Z, 0), pp[:, 2, :], ACTF.Copy).then_inc(vn_done, 1)
            yield
            yield
            yield
            act.wait_ge(vn_mm, 2 * grp + 2)
            act.activation(half(Z, 1), pp[:, 1, :], ACTF.Copy).then_inc(vn_done, 1)
            yield
            yield

        def mixer_pool(pool):
            for grp in range(2):
                for n in range(NL):
                    if n == 0:
                        pool.wait_ge(x1_ready, grp + 1)
                    else:
                        pool.wait_ge(z_mm, grp * NL + n)
                    pool.tensor_tensor(tiles(L), tiles(M), over(level(n + 1), 2 * 4), ALU.mult).then_inc(l_ready, 1)

        done = [0]

        def mixer_dve(dve):
            def step(ins):
                done[0] += 1
                ins.then_inc(dve_step, 1)
                dve.wait_ge(dve_step, done[0])

            dve.wait_ge(gates_lo, 1)
            dve.tensor_tensor(g24[:], pp[0:NG, 0, 0:T], glo[:], ALU.add).then_inc(gates_sum, 1)
            yield
            dve.wait_ge(gates_t, 1)
            dve.tensor_tensor(gt[:], pp[:, 1, 0:64].rearrange("p (c n) -> p c n", c=2)[:, :, 0:NG],
                              over(sm[:, S_BIAS:S_BIAS + NG], NCH), ALU.add).then_inc(gt_ready, 1)
            yield
            dve.wait_ge(gt_act, 1)
            dve.tensor_scalar(ipre[:], th[:, :, 0:HM], CAP, None, ALU.mult)
            dve.wait_ge(gt_ready, 1)
            dve.tensor_copy(spi[:, :, 0:HG], gt[:, :, 0:HG])
            step(dve.tensor_scalar(spi[:, :, HG:HG + HM], th[:, :, HM:2 * HM], -CAP, None, ALU.mult))
            dve.scalar_tensor_tensor(spa[:], spi[:], -1.0, spi[:], ALU.mult, ALU.min).then_inc(sp_in, 1)
            step(dve.tensor_scalar(beta[:], beta[:], 1.0, None, ALU.add))
            step(dve.reciprocal(beta[:], beta[:]))
            yield
            dve.wait_ge(sp_ln, 1)
            step(dve.scalar_tensor_tensor(gl[:], spi[:], 0.0, spa[:], ALU.max, ALU.add))
            dve.scalar_tensor_tensor(gl[:, :, 0:HG], gl[:, :, 0:HG], -1.0, over(rate[:], NCH),
                                     ALU.mult, ALU.mult).then_inc(gl_ready, 1)
            yield
            yield
            dve.wait_ge(cum_mm, 1)
            dve.tensor_copy(cum[:].rearrange("p c n -> p (c n)"), pp[:, 0, 0:NCH * (HG + HM)]).then_inc(gc_ready, 1)
            dve.tensor_copy(gcrow[:], pp[0:HG, 1, 0:T])
            dve.tensor_copy(srow[:], pp[0:HM, 1, T:2 * T])
            dve.memset(crow[:, :, 0:C], 0.0)
            step(dve.tensor_copy(crow[:, 1, C:C + T], pp[0:HM, 0, T:2 * T]))
            dve.tensor_tensor(crow[:, 0, C:C + T], crow[:, 1, C:C + T], srow[:], ALU.add).then_inc(rows_ready, 1)
            for g in range(HG):
                if g == HG // 2:
                    yield
                dve.wait_ge(l2_std, g // 2 + 1)
                scale = float(P) ** -0.5 if g < HG // 2 else 1.0
                dve.scalar_tensor_tensor(qkv[:, 2 * g:2 * g + 2, :], qkv[:, 2 * g:2 * g + 2, :], scale, slot(*sums[g]),
                                         ALU.mult, ALU.mult).then_inc(l2_done, 1)
            dve.wait_ge(gc_ready, 1)
            dve.tensor_tensor(acol[:], ipre[:], cum[:, :, HG:HG + HM], ALU.add)
            dve.wait_ge(eg_done, 1)
            step(dve.scalar_tensor_tensor(egn[:], egn[:], -1.0, beta[:], ALU.mult, ALU.mult))
            dve.wait_ge(rows_ready, 1)
            src, reach = 0, 1
            while reach < T:
                step(dve.tensor_tensor(crow[:, 1 - src, C:C + T], crow[:, src, C:C + T],
                                       crow[:, src, C - reach:C + T - reach], ALU.max))
                src, reach = 1 - src, 2 * reach
            step(dve.tensor_scalar(mrow[:, 0, :], crow[:, src, C:C + T], 0.0, None, ALU.max))
            dve.tensor_tensor(mrow[:, 1, :], srow[:], mrow[:, 0, :], ALU.subtract).then_inc(mrows_ready, 1)
            yield
            dve.wait_ge(mrows_ready, 1)
            for grp in range(2):
                yield from group_dve(dve, grp, step)
            yield
            yield
            for m in range(HM):
                dve.wait_ge(mb_mm, m + 1)
                e = mE[m % 2]
                dve.tensor_scalar(e[:, 0:T], pp[:, 0, 0:T], acol[:, 0, m:m + 1], 0.0, ALU.subtract, ALU.max)
                dve.tensor_scalar(e[:, T:3 * C], pp[:, 0, C:T], acol[:, 1, m:m + 1], 0.0, ALU.subtract,
                                  ALU.max).then_inc(me_pre, 1)
                o = qkv[:, v_at + 2 * m:v_at + 2 * m + 2, :]
                dve.wait_ge(on_std, m // 2 + 1)
                step(dve.tensor_tensor(o, o, slot(*sums[m]), ALU.mult))
                dve.scalar_tensor_tensor(o, o, sm[:, S_GNW:S_GNW + 1], gz_gate(m),
                                         ALU.mult, ALU.mult).then_inc(on_pre, 1)
                diag = e.rearrange("p (a c) -> p a c", a=3)[:, 0:3:2]
                dve.wait_ge(me_exp, m + 1)
                step(dve.tensor_tensor(diag, diag, over(tri, 2), ALU.mult))
                dve.wait_ge(mqk_mm, m + 1)
                dve.scalar_tensor_tensor(mP[m % 2], pp[:, 1, 0:3 * C], float(P) ** -0.5, e, ALU.mult, ALU.mult).then_inc(p_done, 1)
                yield
                dve.wait_ge(on_pre, m + 1)
                dve.wait_ge(mx_exp, m + 1)
                dve.wait_ge(num_mm, m + 1)
                dn = mDn[:, m % 2]
                step(dve.tensor_tensor(dn, pp[:, 1, 0:T], mX[:, m % 2], ALU.max))
                step(dve.scalar_tensor_tensor(dn, pp[:, 1, 0:T], -1.0, dn, ALU.mult, ALU.max))
                step(dve.reciprocal(dn, dn))
                dve.scalar_tensor_tensor(qkv[:, 2 * m:2 * m + 2, :], pp[:, 3, :].rearrange("p (e t) -> p e t", e=2), 0.5,
                                         over(dn, 2), ALU.mult, ALU.mult).then_inc(mh_done, 1)
                yield

        def group_dve(dve, grp, step):
            h0 = 4 * grp
            dve.wait_ge(er_done, grp + 1)
            for c in range(NCH):
                for h in range(4):
                    row, col = pp[:, h // 2, h % 2 * T + c * C:h % 2 * T + (c + 1) * C], cum[:, c, h0 + h:h0 + h + 1]
                    dve.tensor_scalar(DTr[:, c, h], row, col, 0.0, ALU.subtract, ALU.min)
                    ins = dve.tensor_scalar(M[:, c, h], row, col, 0.0, ALU.subtract, ALU.max)
            ins.then_inc(rb_pre, 1)
            yield
            dve.wait_ge(dec_exp, grp + 1)
            dve.tensor_tensor(tiles(M), tiles(M), over(low, 8), ALU.mult)
            step(dve.tensor_tensor(tiles(DTr), tiles(DTr), over(tri, 8), ALU.mult))
            step(dve.tensor_copy(dcol[:], DTr[:, 0, :, C - 1]))
            dve.wait_ge(qk_mm, grp + 1)
            for c in range(NCH):
                ins = dve.tensor_tensor(half(DTr, c), pp[:, 2 + c, :], half(DTr, c), ALU.mult)
            ins.then_inc(at_done, 1)
            yield
            dve.wait_ge(kk_mm, grp + 1)
            for c in range(NCH):
                for h in range(4):
                    ins = dve.scalar_tensor_tensor(M[:, c, h], bank(c, h), beta[:, c, h0 + h:h0 + h + 1], M[:, c, h],
                                                   ALU.mult, ALU.mult)
            ins.then_inc(m_done, 1)
            dve.wait_ge(m_done, grp + 1)
            step(dve.tensor_tensor(tiles(L), tiles(M), over(level(0), 8), ALU.mult))
            dve.tensor_tensor(tiles(X), over(ident, 8), tiles(L), ALU.subtract).then_inc(x1_ready, 1)
            yield
            dve.wait_ge(kt_mm, grp + 1)
            for h in range(4):
                ins = dve.tensor_scalar(KD[:, h], bank(0, h), dcol[:, h:h + 1], None, ALU.mult)
            ins.then_inc(kd_done, 1)
            dve.wait_ge(vt_mm, grp + 1)
            for h in range(4):
                dve.tensor_scalar(R[:, 0, h], bank(2, h), beta[:, 0, h0 + h:h0 + h + 1], None, ALU.mult)
                ins = dve.tensor_scalar(V1[:, h], bank(3, h), beta[:, 1, h0 + h:h0 + h + 1], None, ALU.mult)
            ins.then_inc(v_done, 1)
            yield
            yield
            for n in range(NL):
                if grp and n < 4:
                    dve.wait_ge(gz_tanh, 1)
                    dve.scalar_tensor_tensor(gz_gate(n), gz_gate(n), 1.0, rest[:, gz_at + 2 * n:gz_at + 2 * n + 2, :],
                                             ALU.add, ALU.mult).then_inc(gz_done, 1)
                yield
                dve.wait_ge(yz_mm, grp * NL + n + 1)
                if n == 0:
                    dve.wait_ge(y1_done, grp + 1)
                for c in range(NCH):
                    ins = dve.tensor_tensor(half(Y, c), half(Y, c), pp[:, c, :], ALU.subtract)
                ins.then_inc(y_done, 1)
                if n < NL - 1:
                    dve.wait_ge(xz_mm, grp * (NL - 1) + n + 1)
                    for c in range(NCH):
                        ins = dve.tensor_tensor(half(X, c), half(X, c), pp[:, 2 + c, :], ALU.subtract)
                    ins.then_inc(x_done, 1)
                yield
            dve.wait_ge(z_mm, (grp + 1) * NL)
            dve.tensor_tensor(L[:, 1], qkv[:, q_at + h0:q_at + h0 + 4, C:T], ER[:], ALU.mult).then_inc(qd_done, 1)
            yield
            dve.wait_ge(s1_mm, grp + 1)
            dve.tensor_copy(half(L, 0), pp[:, 3, :]).then_inc(s1_done, 1)
            yield
            dve.wait_ge(ks_mm, grp + 1)
            for h in range(4):
                ins = dve.scalar_tensor_tensor(R[:, 1, h], bank(0, h), egn[:, 1, h0 + h:h0 + h + 1], V1[:, h],
                                               ALU.mult, ALU.add)
            ins.then_inc(r1_done, 1)
            dve.wait_ge(o_mm, 2 * grp + 1)
            copy_out(dve, h0, 0)
            yield
            yield
            dve.wait_ge(o_mm, 2 * grp + 2)
            copy_out(dve, h0, 1)
            yield

        def copy_out(dve, h0, c):
            o = qkv[:, v_at + h0:v_at + h0 + 4, c * C:(c + 1) * C]
            dve.tensor_copy(o, pp[:, 2 + c, :].rearrange("p (h c) -> p h c", h=4)).then_inc(o_done, 1)

        def finish_act(act):
            act.wait_ge(unit_done, SLOTS + plan["out"][0])
            for p in range(pairs):
                act.wait_ge(on_pre, p + 1)
                act.activation(xs[:, 2 * p:2 * p + 2, 0:T], qkv[:, v_at + 2 * p:v_at + 2 * p + 2, :], ACTF.Copy).then_inc(on_hi, 1)
                act.wait_ge(bank_free, 2 + mv_jobs + p + 1)
                mo = rest[:, mo_at + 2 * p:mo_at + 2 * p + 2, :]
                act.activation(mo, mo, ACTF.Tanh, scale=0.5).then_inc(mo_tanh, 1)
            for m in range(HM):
                act.wait_ge(my_pre, m + 1)
                act.activation(xs[:, HG + 2 * m:HG + 2 * m + 2, 0:T], mY[m % 2], ACTF.Copy).then_inc(my_hi, 1)

        def finish_dve(dve):
            for p in range(pairs):
                dve.wait_ge(on_hi, p + 1)
                dve.tensor_tensor(xs[:, 2 * p:2 * p + 2, T:2 * T], qkv[:, v_at + 2 * p:v_at + 2 * p + 2, :],
                                  xs[:, 2 * p:2 * p + 2, 0:T].bitcast(F32), ALU.subtract).then_inc(y_split, 1)
            for m in range(HM):
                dve.wait_ge(mo_tanh, m + 1)
                dve.wait_ge(mh_done, m + 1)
                if m >= 2:
                    dve.wait_ge(y_split, pairs + m - 1)
                dve.scalar_tensor_tensor(mY[m % 2], rest[:, mo_at + 2 * m:mo_at + 2 * m + 2, :], 1.0,
                                         qkv[:, 2 * m:2 * m + 2, :], ALU.add, ALU.mult).then_inc(my_pre, 1)
                dve.wait_ge(my_hi, m + 1)
                x2 = slice(HG + 2 * m, HG + 2 * m + 2)
                dve.tensor_tensor(xs[:, x2, T:2 * T], mY[m % 2], xs[:, x2, 0:T].bitcast(F32), ALU.subtract).then_inc(y_split, 1)

        block = ctx.enter_context(nc.Block())

        @block.sync
        def _(sp):
            x_dram = x.rearrange("(k p) t -> p k t", p=P)
            for q in range(4):
                sp.dma_start(res[:, 4 * q:4 * q + 4, :], x_dram[:, 4 * q:4 * q + 4, :]).then_inc(x_in[q], 16)
            sp.dma_start(sm[:], small).then_inc(small_in, 16)
            with sp.Fori(0, UNITS // STAGES) as i:
                for s in range(STAGES):
                    sp.wait_ge(split, i * STAGES + (s + 1))
                    sp.dma_start(st[:, s].rearrange("p k n -> p (k n)"),
                                 stream[bass.ds(i * STAGES + s, 1)].rearrange("u p n -> (u p) n")).then_inc(staged[s], 16)
            for q in range(DT_ // 4):
                sp.wait_ge(t_ready, 3 * DT_ // 4 + q + 1)
                sp.dma_start(out[q * 4 * P:(q + 1) * 4 * P, :].rearrange("(k p) t -> p k t", p=P),
                             nt[:, q % 2]).then_inc(out_done[q % 2], 16)
            for b in range(2):
                sp.wait_ge(out_done[b], 16 * (DT_ // 8))

        @block.gpsimd
        def _(pool):
            pool.wait_ge(unit_done, SLOTS + 4)
            pool.dma_start(kc[:], consts).then_inc(consts_in, 16)
            pool.wait_ge(unit_done, SLOTS + U_FFN)
            pool.dma_start(wgf[:].rearrange("p k n -> p (k n)"), wg).then_inc(wg_in, 16)
            mixer_pool(pool)

        @block.tensor
        def _(pe):
            def job(i, name, jj, rhs, before_unit, side):
                u0, j0, per, n_units, _ = plan[name]
                pe.wait_ge(bank_free, i * per + (j0 + jj + 1))
                for u in range(n_units):
                    g = jj * n_units + u
                    s = g % SLOTS
                    pe.wait_ge(split, i * (per * n_units) + (STAGES + u0 + g + 1))
                    before_unit(jj, u)
                    for n in range(2):
                        for k in range(UK):
                            kt, last = u * UK + k, u == n_units - 1 and k == UK - 1
                            cols = slice(n * P, (n + 1) * P)
                            pe.matmul(pg[:, jj % 2, n, :], whi[:, s, k, cols], rhs[:, kt, :],
                                      start=u == 0 and k == 0, stop=False, skip_group_check=True)
                            mm = pe.matmul(pg[:, jj % 2, n, 0:T], wlo[:, s, k, cols], rhs[:, kt, 0:T],
                                           start=False, stop=last, skip_group_check=True)
                    mm.then_inc(unit_done, 1)
                    next(side, None)

            def phase(name, rhs, before_unit, side=iter(())):
                for i in rounds_of(pe, name):
                    for jj in range(plan[name][2]):
                        job(i, name, jj, rhs, before_unit, side)

            def after_norm(n):
                def before(jj, u):
                    if jj == 0:
                        pe.wait_ge(x_ready, n * DT_ // 4 + u + 1)
                return before

            def after_blocks(first):
                def before(jj, u):
                    if jj == 0:
                        pe.wait_ge(h_split, 1 + first + UK // 2 * (u + 1))
                return before

            def after_mixer(jj, u):
                if jj == 0:
                    pe.wait_ge(y_split, 2 * (u + 1))

            def total_squares(n):
                pe.wait_ge(ssq_part, n * (NJD + 1))
                pe.matmul(pp[:, 0, 0:T], ones_t[:], ssq[:, 0, :], start=True, stop=False)
                pe.matmul(pp[:, 0, 0:T], ones_t[:], ssq[:, 1, :], start=False, stop=True).then_inc(ssq_mm, 1)

            def ffn(n, norm, block0):
                phase(f"ffn{n}_up_a", xs, after_norm(norm))
                phase(f"ffn{n}_down_a", hs, after_blocks(block0))
                phase(f"ffn{n}_up_b", xs, after_norm(norm))
                phase(f"ffn{n}_down_b", hs, after_blocks(block0 + BLK_A))

            pe.sem_inc(unit_done, SLOTS)
            pe.wait_ge(fills, 2)
            for q in range(4):
                pe.wait_ge(x_sq, q + 1)
                for k in range(4):
                    mm = pe.matmul(pp[:, 0, 0:T], ones_t[:], nt[:, q % 2, k], start=q == 0 and k == 0, stop=q == 3 and k == 3)
                mm.then_inc(x_sq_mm, 1)
            ffn(1, 0, 0)
            total_squares(1)
            phase("in_qkv", xs, after_norm(1))
            side = mixer_pe(pe)
            phase("in_rest", xs, after_norm(1), side)
            for _ in side:
                pass
            phase("out", xs, after_mixer)
            total_squares(2)
            ffn(2, 2, BLK_A + BLK_B)
            total_squares(3)

        @block.scalar
        def _(act):
            def split_unit(i, per_round, g):
                if isinstance(i, int) and i * per_round + g >= UNITS:
                    return
                s = g % SLOTS
                act.wait_ge(staged[s], i * (16 * per_round // STAGES) + 16 * (g // STAGES + 1))
                act.wait_ge(unit_done, i * per_round + (g + 1))
                act.activation(whi[:, s], st[:, s], ACTF.Copy).then_inc(hi_ready, 1)

            def phase(name, scale, finish, side=iter(())):
                u0, j0, per, n_units, rounds = plan[name]
                late = 1 if name == "in_rest" else 2
                for i in rounds_of(act, name):
                    for jj in range(per):
                        first = u0 + jj * n_units + SLOTS
                        for u in range(n_units - late):
                            split_unit(i, per * n_units, first + u)
                            next(side, None)
                        act.wait_ge(unit_done, i * (per * n_units) + (SLOTS + u0 + (jj + 1) * n_units))
                        act.activation(tmp[:, jj % 2], pg[:, jj % 2, :, T:2 * T], ACTF.Copy, scale=scale).then_inc(lo_copied, 1)
                        for u in range(n_units - late, n_units):
                            split_unit(i, per * n_units, first + u)
                            next(side, None)
                        if finish:
                            finish(i, jj)

            def block_finish(name, block0):
                j0 = plan[name][1]
                def finish(i, jj):
                    if jj == 0:
                        act.wait_ge(bank_free, i * 2 + (2 + j0 + 1))
                        act.activation(sg[:], gsum[:], ACTF.Tanh, scale=0.5).then_inc(gate_tanh, 1)
                    else:
                        act.wait_ge(h_ready, i + (block0 + 1))
                        act.activation(hs[:, bass.ds(i * 2, 2), 0:T], hp[:], ACTF.Copy).then_inc(h_hi, 1)
                return finish

            def residual_finish(name, r0, q0):
                per = plan[name][2]
                def finish(i, jj):
                    act.wait_ge(res_done, i * per + (r0 + jj + 1))
                    act.activation(sq[:], res[:, bass.ds(i * 2 * per + 2 * jj, 2), :],
                                   ACTF.Square).then_inc(sq_done, 1)
                return finish

            def norm(n):
                if n:
                    act.wait_ge(ssq_mm, n)
                else:
                    act.wait_ge(x_sq_mm, 4)
                act.activation(rstd[:], pp[:, 0, 0:T], ACTF.Ln, bias=eps[:], scale=1.0 / D).then_inc(ln_done, 1)
                act.wait_ge(ln_done, n + 1)
                act.activation(rstd[:], rstd[:], ACTF.Exp, scale=-0.5).then_inc(rstd_done, 1)
                if n < 3:
                    for q in range(DT_ // 4):
                        act.wait_ge(t_ready, n * DT_ // 4 + q + 1)
                        act.activation(xs[:, 4 * q:4 * q + 4, 0:T], nt[:, q % 2], ACTF.Copy).then_inc(x_hi, 1)

            def ffn(n, block0, jobs0, squares0):
                phase(f"ffn{n}_up_a", 1.0, block_finish(f"ffn{n}_up_a", block0))
                phase(f"ffn{n}_down_a", 0.5, None)
                phase(f"ffn{n}_up_b", 1.0, block_finish(f"ffn{n}_up_b", block0 + BLK_A))
                phase(f"ffn{n}_down_b", 0.5, residual_finish(f"ffn{n}_down_b", jobs0 + NJD, squares0))

            for q in range(4):
                act.wait_ge(x_in[q], 16)
                if q >= 2:
                    act.wait_ge(x_sq_mm, q - 1)
                act.activation(nt[:, q % 2], res[:, 4 * q:4 * q + 4, :], ACTF.Square).then_inc(x_sq, 1)
            act.wait_ge(fills, 2)
            for g in range(2):
                split_unit(0, 0, g)
            norm(0)
            for g in range(2, SLOTS):
                split_unit(0, 0, g)
            ffn(1, 0, 0, 0)
            norm(1)
            act.wait_ge(wg_in, 16)
            act.activation(wgh[:], wgf[:], ACTF.Copy).then_inc(wg_hi, 1)
            act.wait_ge(fills, 5)

            def qkv_finish(i, jj):
                act.wait_ge(bank_free, i * 2 + (2 + plan["in_qkv"][1] + jj + 1))
                for n in range(2):
                    tap = sm[:, bass.ds(i * (4 * CW) + (S_CONV + (2 * jj + n) * CW + CW - 1), 1)]
                    ins = act.activation(cv[:, n], raw[:, n, CW - 1:CW - 1 + T], ACTF.Copy, scale=tap)
                ins.then_inc(tap0, 1)
                act.wait_ge(conv_step, i * (2 * (CW - 1)) + (jj + 1) * (CW - 1))
                act.activation(cth[:], cv[:], ACTF.Tanh).then_inc(conv_tanh, 1)

            phase("in_qkv", 1.0, qkv_finish)
            side = mixer_act(act)
            phase("in_rest", 1.0, None, side)
            for _ in side:
                pass
            finish_act(act)
            phase("out", 1.0, residual_finish("out", 2 * NJD, NJD))
            norm(2)
            ffn(2, BLK_A + BLK_B, 3 * NJD, 2 * NJD)
            norm(3)

        @block.vector
        def _(dve):
            def split_unit(i, per_round, g):
                if isinstance(i, int) and i * per_round + g >= UNITS:
                    return
                s = g % SLOTS
                dve.wait_ge(hi_ready, i * per_round + (g + 1))
                dve.tensor_tensor(wlo[:, s], st[:, s], whi[:, s].bitcast(F32), ALU.subtract).then_inc(split, 1)

            def phase(name, add, finish, side=iter(())):
                u0, j0, per, n_units, rounds = plan[name]
                late = 1 if name == "in_rest" else 2
                for i in rounds_of(dve, name):
                    for jj in range(per):
                        first = u0 + jj * n_units + SLOTS
                        for u in range(n_units - late):
                            split_unit(i, per * n_units, first + u)
                            next(side, None)
                        dve.wait_ge(lo_copied, i * per + (j0 + jj + 1))
                        add(i, jj, pg[:, jj % 2, :, 0:T], tmp[:, jj % 2]).then_inc(bank_free, 1)
                        for u in range(n_units - late, n_units):
                            split_unit(i, per * n_units, first + u)
                            next(side, None)
                        if finish:
                            finish(i, jj)

            def add_gate_or_up(i, jj, hi, lo):
                if jj == 0:
                    return dve.tensor_tensor(gsum[:], hi, lo, ALU.add)
                return dve.tensor_tensor(usum[:], hi, lo, ALU.add)

            def block_finish(name, block0):
                j0 = plan[name][1]
                def finish(i, jj):
                    if jj == 0:
                        dve.wait_ge(gate_tanh, i + (block0 + 1))
                        dve.scalar_tensor_tensor(sg[:], sg[:], 1.0, gsum[:], ALU.add, ALU.mult).then_inc(gate_act, 1)
                    else:
                        dve.wait_ge(gate_act, i + (block0 + 1))
                        dve.wait_ge(h_split, i + (block0 + 1))
                        dve.wait_ge(bank_free, i * 2 + (2 + j0 + 2))
                        dve.scalar_tensor_tensor(hp[:], sg[:], 0.5, usum[:], ALU.mult, ALU.mult).then_inc(h_ready, 1)
                        dve.wait_ge(h_hi, i + (block0 + 1))
                        t = bass.ds(i * 2, 2)
                        dve.tensor_tensor(hs[:, t, T:2 * T], hp[:], hs[:, t, 0:T].bitcast(F32),
                                          ALU.subtract).then_inc(h_split, 1)
                return finish

            def add_scaled(scale):
                return lambda i, jj, hi, lo: dve.scalar_tensor_tensor(gsum[:], hi, scale, lo, ALU.mult, ALU.add)

            def clear_squares(n):
                dve.memset(ssq[:], 0.0).then_inc(ssq_part, 1)
                dve.wait_ge(ssq_part, (n - 1) * (NJD + 1) + 1)

            def residual_finish(name, r0, q0, n):
                j0, per = plan[name][1:3]
                def finish(i, jj):
                    dve.wait_ge(bank_free, i * per + (2 + j0 + jj + 1))
                    t = bass.ds(i * 2 * per + 2 * jj, 2)
                    dve.tensor_tensor(res[:, t, :], res[:, t, :], gsum[:], ALU.add).then_inc(res_done, 1)
                    dve.wait_ge(res_done, i * per + (r0 + jj + 1))
                    if n is not None:
                        dve.wait_ge(sq_done, i * per + (q0 + jj + 1))
                        dve.tensor_tensor(ssq[:], ssq[:], sq[:], ALU.add).then_inc(ssq_part, 1)
                        dve.wait_ge(ssq_part, i * per + ((n - 1) * (NJD + 1) + 1 + jj + 1))
                return finish

            def norm(n):
                dve.wait_ge(rstd_done, n + 1)
                groups = DT_ // 4

                def remainder(q):
                    dve.wait_ge(x_hi, n * groups + q + 1)
                    dve.tensor_tensor(xs[:, 4 * q:4 * q + 4, T:2 * T], nt[:, q % 2],
                                      xs[:, 4 * q:4 * q + 4, 0:T].bitcast(F32), ALU.subtract).then_inc(x_ready, 1)

                for q in range(groups):
                    if n == 3 and q >= 2:
                        dve.wait_ge(out_done[q % 2], 16 * (q // 2))
                    if n < 3 and q >= 2:
                        dve.wait_ge(x_ready, n * groups + q - 1)
                    for k in range(4 * q, 4 * q + 4):
                        ins = dve.scalar_tensor_tensor(nt[:, q % 2, k % 4], res[:, k, :], w_cols(n, k), rstd[:],
                                                       ALU.mult, ALU.mult)
                    ins.then_inc(t_ready, 1)
                    if n < 3 and q:
                        remainder(q - 1)
                if n < 3:
                    remainder(groups - 1)

            def ffn(n, block0, jobs0, squares0, norm_after):
                phase(f"ffn{n}_up_a", add_gate_or_up, block_finish(f"ffn{n}_up_a", block0))
                phase(f"ffn{n}_down_a", add_scaled(0.5), residual_finish(f"ffn{n}_down_a", jobs0, None, None))
                phase(f"ffn{n}_up_b", add_gate_or_up, block_finish(f"ffn{n}_up_b", block0 + BLK_A))
                clear_squares(norm_after)
                phase(f"ffn{n}_down_b", add_scaled(0.5),
                      residual_finish(f"ffn{n}_down_b", jobs0 + NJD, squares0, norm_after))

            dve.memset(ones_t[:], 1.0).then_inc(fills, 1)
            dve.memset(eps[:], EPS).then_inc(fills, 1)
            dve.sem_inc(split, STAGES)
            dve.sem_inc(bank_free, 2)
            dve.sem_inc(h_split, 1)
            for g in range(2):
                split_unit(0, 0, g)
            dve.wait_ge(small_in, 16)
            norm(0)
            for g in range(2, SLOTS):
                split_unit(0, 0, g)
            ffn(1, 0, 0, 0, 1)
            norm(1)

            dve.tensor_scalar(sm[:, S_CONV:S_GNW + 1], sm[:, S_CONV:S_GNW + 1], 0.5, None, ALU.mult).then_inc(fills, 1)
            dve.memset(raw[:, 0, 0:CW - 1], 0.0).then_inc(fills, 1)
            dve.memset(raw[:, 1, 0:CW - 1], 0.0).then_inc(fills, 1)
            dve.wait_ge(fills, 5)

            def add_qkv(i, jj, hi, lo):
                return dve.tensor_tensor(raw[:, :, CW - 1:CW - 1 + T], hi, lo, ALU.add)

            def qkv_finish(i, jj):
                job = i * 2 + (jj + 1)
                dve.wait_ge(tap0, job)
                for w in range(1, CW):
                    for n in range(2):
                        tap = sm[:, bass.ds(i * (4 * CW) + (S_CONV + (2 * jj + n) * CW + CW - 1 - w), 1)]
                        ins = dve.scalar_tensor_tensor(cv[:, n], raw[:, n, CW - 1 - w:CW - 1 - w + T], tap, cv[:, n],
                                                       ALU.mult, ALU.add)
                    ins.then_inc(conv_step, 1)
                    if w < CW - 1:
                        dve.wait_ge(conv_step, i * (2 * (CW - 1)) + (jj * (CW - 1) + w))
                dve.wait_ge(conv_tanh, job)
                dve.scalar_tensor_tensor(qkv[:, bass.ds(i * 4 + 2 * jj, 2), :], cth[:], 1.0, cv[:],
                                         ALU.add, ALU.mult).then_inc(qkv_done, 1)

            def add_rest(i, jj, hi, lo):
                return dve.tensor_tensor(rest[:, bass.ds(i * 4 + 2 * jj, 2), :], hi, lo, ALU.add)

            dve.wait_ge(wg_hi, 1)
            dve.tensor_tensor(wgl[:], wgf[:], wgh[:].bitcast(F32), ALU.subtract).then_inc(wg_split, 1)
            phase("in_qkv", add_qkv, qkv_finish)
            side = mixer_dve(dve)
            phase("in_rest", add_rest, None, side)
            for _ in side:
                pass
            finish_dve(dve)
            clear_squares(2)
            phase("out", add_scaled(1.0), residual_finish("out", 2 * NJD, NJD, 2))
            norm(2)
            ffn(2, BLK_A + BLK_B, 3 * NJD, 2 * NJD, 3)
            norm(3)


def lay_out(inputs):
    a = {k: np.asarray(v) for k, v in inputs.items()}

    def units(w, rows, cols):
        w = w[rows, cols]
        return w.reshape(w.shape[0] // (UK * P), UK, P, w.shape[1] // UN, UN).transpose(3, 0, 2, 1, 4)

    def flat(u):
        return u.reshape(-1, P, UK * UN)

    def ffn(n):
        gate, up, down = (a[f"ffn{n}_w_{x}"][0] for x in ("gate", "up", "down"))
        parts = []
        for first, blocks in ((0, BLK_A), (BLK_A, BLK_B)):
            f = slice(first * UN, (first + blocks) * UN)
            every = slice(None)
            parts.append(flat(np.stack([units(gate, every, f), units(up, every, f)], axis=1)))
            parts.append(flat(units(down, f, every)))
        return parts

    w_in = a["w_in"][0]
    gqkvz, gab = HG * 4 * P, 2 * HG
    mqkvo = (2 * HM + 2 * 2 * HM) * P
    every = slice(None)
    stream = np.concatenate(
        ffn(1) + [flat(units(w_in, every, slice(0, gqkvz))), flat(units(w_in, every, slice(gqkvz + gab, gqkvz + gab + mqkvo))),
                  flat(units(a["w_out"][0], every, every))] + ffn(2))
    wg = np.concatenate([w_in[:, gqkvz:gqkvz + gab], w_in[:, gqkvz + gab + mqkvo:]], axis=1)
    wg = wg.reshape(DT_, P, NG).transpose(1, 0, 2).reshape(P, DT_ * NG)

    def columns(v):
        return v.reshape(-1, P).T

    def on_all(row):
        return np.broadcast_to(row, (P, row.shape[-1]))

    conv = a["conv_w"][0].reshape(CW, NQKV, P).transpose(2, 1, 0).reshape(P, NQKV * CW)
    bias = np.concatenate([a["gdn_dt_bias"][0], np.zeros(HG, np.float32), a["ml_i_bias"][0], a["ml_f_bias"][0]])
    small = np.concatenate([columns(a["ffn1_norm_w"]), columns(a["mix_norm_w"]), columns(a["ffn2_norm_w"]),
                            columns(a["final_norm_w"]), conv, columns(a["gdn_norm_w"]), on_all(bias),
                            on_all(a["gdn_a_log"][0])], axis=1)
    return {"stream": stream, "x": a["x"][0].T, "wg": wg, "small": small, "consts": constants()}


def kernel(**inputs):
    import concourse.bacc as bacc
    from concourse.bass_utils import run_bass_kernel_spmd as run

    nc = bacc.Bacc("TRN2", target_bir_lowering=False, num_devices=1)
    arrays, args = {}, []
    for name, a in lay_out(inputs).items():
        a = np.ascontiguousarray(a)
        arrays[f"in_{name}_dram"] = a
        args.append(nc.dram_tensor(f"in_{name}_dram", a.shape, mybir.dt.from_np(a.dtype), kind="ExternalInput").ap())
    args.append(nc.dram_tensor("out_0_dram", (D, T), F32, kind="ExternalOutput").ap())
    build(nc, *args)
    r = run(nc, [arrays], core_ids=[0])
    return np.ascontiguousarray(r.results[0]["out_0_dram"].T).reshape(1, T, D)
```

```python
from contextlib import ExitStack

import numpy as np

import concourse.bass as bass
from concourse import mybir

F32 = mybir.dt.float32
F32R = mybir.dt.float32r
ACTF = mybir.ActivationFunctionType
ALU = mybir.AluOpType

P = 128
T = 256
D = 2048
DT_ = D // P
F = 5632
UK = 4
UN = 256
BLK_A, BLK_B = 12, 10
NJD = D // UN
HG, HM = 8, 4
NQKV = 3 * HG
NREST = HG + 2 * HM + 2 * 2 * HM
NG = 2 * HG + 2 * HM
CW = 4
C = 128
NCH = T // C
EPS = 1e-6
CAP = 15.0
STAGES = 4
SLOTS = 4
LEVELS = [1, 2, 4, 8, 16, 32, 64]

U_FFN_BLOCK = 2 * DT_ // UK
U_IN = (NQKV + NREST) // 2 * (DT_ // UK)
U_OUT = NJD * DT_ // UK
U_DOWN_A, U_DOWN_B = 2 * BLK_A // UK, 2 * BLK_B // UK
U_FFN = (BLK_A + BLK_B) * U_FFN_BLOCK + NJD * (U_DOWN_A + U_DOWN_B)
UNITS = 2 * U_FFN + U_IN + U_OUT

S_NORM = 0
S_CONV = S_NORM + 4 * DT_
S_GNW = S_CONV + NQKV * CW
S_BIAS = S_GNW + 1
S_ALOG = S_BIAS + NG
S_N = S_ALOG + HG
K_ID, K_TRI, K_LOW, K_LEV = 0, P, 2 * P, 3 * P
K_N = K_LEV + len(LEVELS) * P


def constants():
    r, c = np.arange(P)[:, None], np.arange(P)[None, :]
    parts = [r == c, c >= r, c < r]
    for b in LEVELS:
        parts.append((r // (2 * b) == c // (2 * b)) & (r // b % 2 == 1) & (c // b % 2 == 0))
    return np.concatenate(parts, axis=1).astype(np.float32)


def build(nc, stream, x, wg, small, consts, out):
    with ExitStack() as ctx:
        base = (nc.sbuf_base + 63) // 64 * 64
        cursor = [base]
        def sb(name, shape, dt, at=None):
            size = int(np.prod(shape[1:])) * 4
            size = (size + 31) // 32 * 32
            if at is None:
                at = cursor[0]
                cursor[0] += size
                assert cursor[0] <= nc.sbuf_usable_end, name
            return nc.alloc_sbuf_tensor_at(name, shape, dt, offset=at), at + size

        def sem(name):
            return ctx.enter_context(nc.semaphore(name))

        st, _ = sb("stage", [P, STAGES, UK, UN], F32)
        whi, _ = sb("w_hi", [P, SLOTS, UK, UN], F32R)
        wlo, _ = sb("w_lo", [P, SLOTS, UK, UN], F32R)
        xs_at = cursor[0]
        xs, _ = sb("x_split", [P, DT_, 2 * T], F32R)
        res, _ = sb("residual", [P, DT_, T], F32)
        hs_at = cursor[0]
        hs, hs_end = sb("h_split", [P, 2 * BLK_A, 2 * T], F32R)
        qkv, _ = sb("qkv", [P, NQKV, T], F32)
        kc, _ = sb("constants", [P, K_N], F32)
        sm, _ = sb("small", [P, S_N], F32)
        rstd, _ = sb("rstd", [P, T], F32)
        ssq, _ = sb("sum_sq", [P, 2, T], F32)
        ones_t, _ = sb("ones", [P, P], F32)
        ones = ones_t[:]
        eps, _ = sb("eps", [P, 1], F32)
        warm, _ = sb("first_use_of_act", [P, 1], F32)
        tmp, _ = sb("low_part", [P, 2, 2, T], F32)
        both = cursor[0]
        gsum, at = sb("gate_sum", [P, 2, T], F32)
        sg, at = sb("gate_silu", [P, 2, T], F32)
        usum, at = sb("up_sum", [P, 2, T], F32)
        hp, at = sb("h_full", [P, 2, T], F32)
        sq, at = sb("squares", [P, 2, T], F32)
        ffn_end = at
        xq, _ = sb("x_squares", [P, DT_, T], F32, at=hs_at)
        fin, _ = sb("result", [P, DT_, T], F32, at=xs_at)
        rest, at = sb("rest", [P, NREST, T], F32, at=hs_at)
        tail = at
        X, at = sb("inv_x", [P, NCH, 4, C], F32, at=at)
        Y, at = sb("inv_y", [P, NCH, 4, C], F32, at=at)
        Z, at = sb("inv_z", [P, NCH, 4, C], F32, at=at)
        L, at = sb("inv_l", [P, NCH, 4, C], F32, at=at)
        assert at <= hs_end
        wgf, _ = sb("wgate", [P, DT_, NG], F32, at=at - 4 * NCH * C * 4)
        raw, at = sb("conv_in", [P, 2, CW - 1 + T], F32, at=tail)
        cv, at = sb("conv_half", [P, 2, T], F32, at=at)
        cth, at = sb("conv_tanh", [P, 2, T], F32, at=at)
        M, at = sb("coupling", [P, NCH, 4, C], F32, at=both)
        DTr, at = sb("decay_t", [P, NCH, 4, C], F32, at=at)
        rhs_at = at
        R, at = sb("rhs_v", [P, NCH, 4, C], F32, at=at)
        V1, at = sb("v_tok1", [P, 4, C], F32, at=at)
        KD, at = sb("k_dec", [P, 4, C], F32, at=at)
        ER, at = sb("exp_gc_row1", [P, 4, C], F32, at=at)
        gcrow, at = sb("gc_rows", [HG, T], F32, at=at)
        mrow, at = sb("m_rows", [HM, 2, T], F32, at=at)
        gt, at = sb("gates_tok", [P, NCH, NG], F32, at=at)
        th, at = sb("tanh", [P, NCH, 2 * HM], F32, at=at)
        beta, at = sb("beta", [P, NCH, HG], F32, at=at)
        ipre, at = sb("i_pre", [P, NCH, HM], F32, at=at)
        spi, at = sb("softplus_in", [P, NCH, HG + HM], F32, at=at)
        spa, at = sb("softplus_abs", [P, NCH, HG + HM], F32, at=at)
        gl, at = sb("g_and_neg_logf", [P, NCH, HG + HM], F32, at=at)
        rate, at = sb("decay_rate", [P, HG], F32, at=at)
        cum, at = sb("cum_cols", [P, NCH, HG + HM], F32, at=at)
        egn, at = sb("neg_exp_gc", [P, NCH, HG], F32, at=at)
        acol, at = sb("a_cols", [P, NCH, HM], F32, at=at)
        dcol, at = sb("decay_to_end", [P, 4], F32, at=at)
        cursor[0] = max(ffn_end, at)
        glo, at = sb("gates_low", [NG, T], F32, at=both)
        g24, at = sb("gates_rows", [NG, T], F32, at=at)
        srow, at = sb("s_rows", [HM, T], F32, at=rhs_at)
        arow, at = sb("a_rows", [HM, T], F32, at=at)
        wgh, _ = sb("wgate_hi", [P, DT_, NG], F32R)
        wgl, _ = sb("wgate_lo", [P, DT_, NG], F32R)

        pg = ctx.enter_context(nc.psum_tensor("gemm_banks", [P, 2, 2, 512], F32))
        pp = ctx.enter_context(nc.psum_tensor("side_banks", [P, 4, 512], F32))

        ident = kc[:, K_ID:K_ID + P]
        tri, low = kc[:, K_TRI:K_TRI + P], kc[:, K_LOW:K_LOW + P]

        def level(n):
            return kc[:, K_LEV + n * P:K_LEV + (n + 1) * P]

        def row_to_all(n, h):
            return kc[0:n, K_ID + h:K_ID + h + 1].to_broadcast([n, P])

        def over(ap, n):
            return ap.rearrange("p (a m) -> p a m", a=1).to_broadcast([ap.shape[0], n, ap.shape[1]])

        small_in = sem("small_landed")
        consts_in = sem("constants_landed")
        wg_in = sem("wgate_landed")
        x_in = [sem(f"x_landed_{q}") for q in range(4)]
        staged = [sem(f"unit_landed_{s}") for s in range(STAGES)]
        hi_ready = sem("hi_ready")
        split = sem("unit_split")
        unit_done = sem("unit_done")
        bank_free = sem("bank_free")
        lo_copied = sem("lo_copied")
        gate_tanh = sem("gate_tanh")
        gate_act = sem("gate_activated")
        h_ready = sem("h_ready")
        h_hi = sem("h_hi_ready")
        h_split = sem("h_split_ready")
        res_done = sem("residual_updated")
        sq_done = sem("squares_ready")
        ssq_part = sem("sum_sq_added")
        x_sq = sem("x_squares_ready")
        ssq_mm = sem("sum_sq_total")
        x_sq_sum = sem("x_squares_sum")
        ln_done = sem("ln_sum_sq")
        rstd_done = sem("rstd_ready")
        normed = sem("sum_normed")
        x_hi = sem("x_hi_ready")
        x_ready = sem("x_split_ready")
        gained = sem("final_gain_applied")
        t_ready = sem("final_norm_ready")
        fills = sem("constants_filled")
        wg_hi = sem("wgate_hi_ready")
        wg_split = sem("wgate_split")
        tap0 = sem("conv_tap0")
        conv_step = sem("conv_step")
        conv_tanh = sem("conv_tanh")
        qkv_done = sem("qkv_done")
        out_done = [sem(f"out_landed_{b}") for b in range(2)]

        def w_cols(n, tile):
            return sm[:, bass.ds(tile + (S_NORM + n * DT_), 1)]


        plan, normed0, u, j, m = {}, {}, 0, 0, 0
        for name, jobs, per, n_units, rounds in [
            ("ffn1_up_a", 2 * BLK_A, 2, DT_ // UK, BLK_A), ("ffn1_down_a", NJD, 2, U_DOWN_A, NJD // 2),
            ("ffn1_up_b", 2 * BLK_B, 2, DT_ // UK, BLK_B), ("ffn1_down_b", NJD, 4, U_DOWN_B, NJD // 4),
            ("in_qkv", NQKV // 2, 2, DT_ // UK, NQKV // 4), ("in_rest", NREST // 2, 2, DT_ // UK, NREST // 4),
            ("out", NJD, 2, DT_ // UK, NJD // 2),
            ("ffn2_up_a", 2 * BLK_A, 2, DT_ // UK, BLK_A), ("ffn2_down_a", NJD, 2, U_DOWN_A, NJD // 2),
            ("ffn2_up_b", 2 * BLK_B, 2, DT_ // UK, BLK_B), ("ffn2_down_b", NJD, 4, U_DOWN_B, NJD // 4),
        ]:
            assert per * rounds == jobs and per * n_units % SLOTS == 0 and u % SLOTS == 0 and j % 2 == 0
            plan[name] = (u, j, per, n_units, rounds)
            u, j = u + jobs * n_units, j + jobs
            if "up" in name or "in" in name:
                normed0[name] = m
                m += jobs
        assert u == UNITS
        norm_of = {"ffn1_up_a": 0, "in_qkv": 1, "ffn2_up_a": 2}

        def rounds_of(eng, name):
            rounds = plan[name][4]
            if name in ("ffn2_down_b", "in_rest"):
                yield from range(rounds)
            elif name in norm_of:
                yield 0
                with eng.Fori(1, rounds) as i:
                    yield i
            else:
                with eng.Fori(0, rounds) as i:
                    yield i

        gates_mm, gates_lo, gates_sum, gates_t = sem("gates_mm"), sem("gates_low"), sem("gates_sum"), sem("gates_turned")
        gt_ready, gt_act, sp_in, sp_ln = sem("gates_biased"), sem("gates_tanh_exp"), sem("softplus_in"), sem("softplus_ln")
        gl_ready, cum_mm, rows_ready, gc_ready = sem("g_ready"), sem("cum_sums_mm"), sem("rows_ready"), sem("gc_cols_ready")
        eg_done = sem("exp_gc_done")
        l2_sq, l2_mm, l2_ln, l2_std, l2_done = sem("l2_squares"), sem("l2_sums"), sem("l2_ln"), sem("l2_rstd"), sem("l2_done")
        rb_mm, rb_diff, rb_pre, er_done, dec_exp, dtr_done, m_low = sem("gc_on_all_mm"), sem("gc_minus_gc"), sem("gc_differences"), sem("exp_gc_row"), sem("decay_exp"), sem("decay_t_masked"), sem("decay_masked")
        qk_mm, at_done, kk_mm, m_done = sem("qk_mm"), sem("attn_done"), sem("kk_mm"), sem("coupling_done")
        vt_mm, v_done, kt_mm, kd_done = sem("v_turned"), sem("v_scaled"), sem("k_turned"), sem("k_dec_done")
        x1_ready, y1_mm, y1_done = sem("x1_ready"), sem("x1_turned"), sem("y1_copied")
        y_done, x_done = sem("y_updated"), sem("x_updated")
        l_ready, z_mm, z_done = sem("l_masked"), sem("z_mm"), sem("z_copied")
        yz_mm, xz_mm = sem("yz_mm"), sem("xz_mm")
        vn_mm, vn_done = sem("v_new_mm"), sem("v_new_copied")
        s1_mm, s1_done, ks_mm, r1_done, qd_done = sem("state_mm"), sem("state_copied"), sem("k_state_mm"), sem("r1_done"), sem("q_dec_done")
        o_mm, o_done = sem("o_mm"), sem("o_copied")
        gz_tanh, gz_done = sem("gz_tanh"), sem("gz_gate_done")
        on_sq, on_mm, on_ln, on_std, on_scaled, on_pre, on_hi = (sem("o_squares"), sem("o_sums"), sem("o_ln"), sem("o_rstd"),
                                                                 sem("o_scaled"), sem("o_gated"), sem("y_hi"))
        y_split = sem("y_split_ready")
        mb_mm, me_pre, me_exp, mx_exp = sem("m_on_all_mm"), sem("m_differences"), sem("m_weights_exp"), sem("m_floor_exp")
        mqk_mm, p_done, mv_mm, mvt_done = sem("m_qk_mm"), sem("p_done"), sem("m_v_turned"), sem("m_v_copied")
        num_mm, den_read, mh_done = sem("m_num_mm"), sem("m_den_read"), sem("m_h_done")
        mo_tanh, my_pre, my_hi = sem("mo_tanh"), sem("m_gated"), sem("m_y_hi")
        dve_step = sem("dve_step")
        act_step = sem("act_step")

        NL = len(LEVELS) - 1
        pairs = HG // 2
        q_at, k_at, v_at = 0, HG, 2 * HG
        gz_at, mq_at, mk_at, mv_at, mo_at = 0, HG, HG + HM, HG + 2 * HM, HG + 4 * HM
        mv_jobs = normed0["in_rest"] + mo_at // 2

        def half(buf, n):
            return buf[:, n].rearrange("p h c -> p (h c)")

        def slot(buf, n):
            return half(buf, n).rearrange("p (a t) -> p a t", a=2)

        def tiles(buf):
            return buf[:].rearrange("p n h c -> p (n h) c")

        def chunk(buf, tile, c):
            return buf[:, tile, c * C:(c + 1) * C]

        def every_second(ap, n, odd):
            return ap.rearrange("p (m s b) -> p m s b", s=2, b=LEVELS[n + 1])[:, :, odd]

        def bank(b, h):
            return pp[:, b, h * C:(h + 1) * C]

        def gz_gate(p):
            at = (q_at if p < 2 else k_at) + p % 2 * 2
            return qkv[:, at:at + 2, :]

        sums = [(buf, n) for buf in (X, Y, Z, L) for n in range(2)]
        mE = [half(DTr, n)[:, 0:3 * C] for n in range(2)]
        mP = [half(M, n)[:, 0:3 * C] for n in range(2)]
        mV = [Z[:, n] for n in range(2)]
        mX = half(L, 0).rearrange("p (a t) -> p a t", a=2)
        mDn = half(L, 1).rearrange("p (a t) -> p a t", a=2)
        mY = [slot(R, n) for n in range(2)]

        def y_pairs(m):
            return {0: [0], 1: [1], 2: [], 3: [2, 3]}[m]

        def mixer_pe(pe):
            pe.wait_ge(wg_split, 1)
            for k in range(DT_):
                pe.matmul(pp[0:NG, 0, :], wgh[:, k, :], xs[:, k, :], start=k == 0, stop=False, skip_group_check=True)
                mm = pe.matmul(pp[0:NG, 0, 0:T], wgl[:, k, :], xs[:, k, 0:T], start=False, stop=k == DT_ - 1,
                               skip_group_check=True)
            mm.then_inc(gates_mm, 1)
            pe.wait_ge(consts_in, 16)
            yield
            for g in range(HG):
                if g == 0:
                    pe.wait_ge(gates_sum, 1)
                    for c in range(NCH):
                        mm = pe.transpose(pp[:, 1, c * 32:c * 32 + NG], g24[:, c * C:(c + 1) * C], ident[0:NG, 0:NG])
                    mm.then_inc(gates_t, 1)
                pe.wait_ge(l2_sq, g + 1)
                if g >= 2:
                    pe.wait_ge(l2_ln, g - 1)
                pe.matmul(pp[:, 2 + g % 2, :], ones, half(*sums[g]), start=True, stop=True).then_inc(l2_mm, 1)
                if g % 2:
                    yield
            pe.wait_ge(gl_ready, 1)
            n = HG + HM
            for c in range(NCH):
                pe.matmul(pp[:, 0, c * n:(c + 1) * n], tri, gl[:, c, :], start=True, stop=True, skip_group_check=True)
            pe.matmul(pp[:, 0, n + HG:2 * n], ones, gl[:, 0, HG:n], start=False, stop=True, skip_group_check=True)
            for c in range(NCH):
                pe.matmul(pp[0:HG, 1, c * C:(c + 1) * C], gl[:, c, 0:HG], tri, start=True, stop=True, skip_group_check=True)
            for c in range(NCH):
                pe.matmul(pp[0:HM, 0, T + c * C:T + (c + 1) * C], ipre[:, c, :], ident, start=True, stop=True,
                          skip_group_check=True)
            for c in range(NCH):
                mm = pe.matmul(pp[0:HM, 1, T + c * C:T + (c + 1) * C], gl[:, c, HG:n], tri, start=True, stop=True,
                               skip_group_check=True)
            mm = pe.matmul(pp[0:HM, 1, T + C:2 * T], gl[:, 0, HG:n], ones, start=False, stop=True, skip_group_check=True)
            mm.then_inc(cum_mm, 1)
            yield
            yield
            yield
            pe.wait_ge(rows_ready, 1)
            for grp in range(2):
                yield from group_pe(pe, grp)
            for p in range(pairs):
                pe.wait_ge(on_sq, p + 1)
                if p >= 2:
                    pe.wait_ge(on_ln, p - 1)
                pe.matmul(pp[:, 2 + p % 2, :], ones, half(*sums[p]), start=True, stop=True).then_inc(on_mm, 1)
                if p % 2:
                    yield
            pe.wait_ge(on_ln, pairs)
            pe.wait_ge(normed, mv_jobs)
            def m_on_all(m):
                pe.matmul(pp[:, 0, :], row_to_all(HM, m), mrow[:].rearrange("h a t -> h (a t)"),
                          start=True, stop=True).then_inc(mb_mm, 1)

            m_on_all(0)
            for m in range(HM):
                for c in range(NCH):
                    for e in range(2):
                        mm = pe.transpose(pp[:, 2, (2 * c + e) * C:(2 * c + e + 1) * C],
                                          chunk(rest, mv_at + 2 * m + e, c), ident)
                mm.then_inc(mv_mm, 1)
                if m:
                    pe.wait_ge(den_read, m)
                q, k = rest[:, mq_at + m], rest[:, mk_at + m]
                pe.matmul(pp[:, 1, 0:T], k[:, 0:C], q, start=True, stop=True, skip_group_check=True)
                pe.matmul(pp[:, 1, T:T + C], k[:, C:T], q[:, C:T], start=True, stop=True,
                          skip_group_check=True).then_inc(mqk_mm, 1)
                yield
                pe.wait_ge(p_done, m + 1)
                pe.wait_ge(mvt_done, m + 1)
                if m:
                    pe.wait_ge(mh_done, m)
                v, w = mV[m % 2], mP[m % 2]
                for e in range(2):
                    pe.matmul(pp[:, 3, e * T:(e + 1) * T], v[:, e], w[:, 0:T], start=True, stop=False, skip_group_check=True)
                    pe.matmul(pp[:, 3, e * T + C:(e + 1) * T], v[:, 2 + e], w[:, T:3 * C], start=False, stop=True,
                              skip_group_check=True)
                pe.matmul(pp[:, 1, 0:T], ones, w[:, 0:T], start=True, stop=False, skip_group_check=True)
                pe.matmul(pp[:, 1, C:T], ones, w[:, T:3 * C], start=False, stop=True,
                          skip_group_check=True).then_inc(num_mm, 1)
                if m + 1 < HM:
                    m_on_all(m + 1)
                yield

        def group_pe(pe, grp):
            h0 = 4 * grp
            q = lambda h, c: chunk(qkv, q_at + h0 + h, c)
            k = lambda h, c: chunk(qkv, k_at + h0 + h, c)
            v = lambda h, c: chunk(qkv, v_at + h0 + h, c)
            if grp:
                pe.wait_ge(o_done, 2 * grp)
            for h in range(4):
                mm = pe.matmul(pp[:, h // 2, h % 2 * T:(h % 2 + 1) * T], row_to_all(HG, h0 + h), gcrow[:],
                               start=True, stop=True, skip_group_check=True)
            mm.then_inc(rb_mm, 1)
            pe.wait_ge(l2_done, HG)
            for c in range(NCH):
                for h in range(4):
                    mm = pe.matmul(bank(2 + c, h), k(h, c), q(h, c), start=True, stop=True, skip_group_check=True)
            mm.then_inc(qk_mm, 1)
            yield
            pe.wait_ge(rb_diff, grp + 1)
            pe.wait_ge(er_done, grp + 1)
            for c in range(NCH):
                for h in range(4):
                    mm = pe.matmul(bank(c, h), k(h, c), k(h, c), start=True, stop=True, skip_group_check=True)
            mm.then_inc(kk_mm, 1)
            yield
            pe.wait_ge(at_done, grp + 1)
            for c in range(NCH):
                for h in range(4):
                    mm = pe.transpose(bank(2 + c, h), v(h, c), ident)
            mm.then_inc(vt_mm, 1)
            yield
            pe.wait_ge(m_done, grp + 1)
            for h in range(4):
                mm = pe.transpose(bank(0, h), k(h, 0), ident)
            mm.then_inc(kt_mm, 1)
            yield
            pe.wait_ge(x1_ready, grp + 1)
            pe.wait_ge(kd_done, grp + 1)
            for c in range(NCH):
                for h in range(4):
                    mm = pe.transpose(bank(c, h), X[:, c, h], ident)
            mm.then_inc(y1_mm, 1)
            yield
            for n in range(NL):
                pe.wait_ge(l_ready, grp * NL + n + 1)
                if n == 0:
                    pe.wait_ge(y1_done, grp + 1)
                    pe.wait_ge(v_done, grp + 1)
                else:
                    pe.wait_ge(y_done, grp * NL + n)
                    pe.wait_ge(x_done, grp * (NL - 1) + n)
                for c in range(NCH):
                    for h in range(4):
                        mm = pe.matmul(bank(2 + c, h), L[:, c, h], Y[:, c, h], start=True, stop=True, skip_group_check=True)
                mm.then_inc(z_mm, 1)
                yield
                pe.wait_ge(z_done, grp * NL + n + 1)
                for c in range(NCH):
                    for h in range(4):
                        mm = pe.matmul(every_second(bank(c, h), n, 1), X[:, c, h], every_second(Z[:, c, h], n, 1),
                                       start=True, stop=True, skip_group_check=True)
                mm.then_inc(yz_mm, 1)
                if n < NL - 1:
                    for c in range(NCH):
                        for h in range(4):
                            mm = pe.matmul(every_second(bank(2 + c, h), n, 0), Z[:, c, h], every_second(X[:, c, h], n, 0),
                                           start=True, stop=True, skip_group_check=True)
                    mm.then_inc(xz_mm, 1)
                yield
            pe.wait_ge(y_done, (grp + 1) * NL)
            for h in range(4):
                mm = pe.matmul(bank(2, h), Y[:, 0, h], R[:, 0, h], start=True, stop=True, skip_group_check=True)
            mm.then_inc(vn_mm, 1)
            yield
            pe.wait_ge(vn_done, 2 * grp + 1)
            for h in range(4):
                mm = pe.matmul(bank(3, h), KD[:, h], Z[:, 0, h], start=True, stop=True, skip_group_check=True)
            mm.then_inc(s1_mm, 1)
            for h in range(4):
                mm = pe.matmul(bank(2, h), Z[:, 0, h], DTr[:, 0, h], start=True, stop=True, skip_group_check=True)
            mm.then_inc(o_mm, 1)
            yield
            pe.wait_ge(s1_done, grp + 1)
            for h in range(4):
                mm = pe.matmul(bank(0, h), k(h, 1), L[:, 0, h], start=True, stop=True, skip_group_check=True)
            mm.then_inc(ks_mm, 1)
            yield
            pe.wait_ge(r1_done, grp + 1)
            for h in range(4):
                mm = pe.matmul(bank(1, h), Y[:, 1, h], R[:, 1, h], start=True, stop=True, skip_group_check=True)
            mm.then_inc(vn_mm, 1)
            yield
            pe.wait_ge(qd_done, grp + 1)
            pe.wait_ge(vn_done, 2 * grp + 2)
            for h in range(4):
                pe.matmul(bank(3, h), L[:, 0, h], L[:, 1, h], start=True, stop=False, skip_group_check=True)
                mm = pe.matmul(bank(3, h), Z[:, 1, h], DTr[:, 1, h], start=False, stop=True, skip_group_check=True)
            mm.then_inc(o_mm, 1)
            yield

        def mixer_act(act):
            act.wait_ge(qkv_done, NQKV // 2)
            def square(g):
                act.activation(slot(*sums[g]), qkv[:, 2 * g:2 * g + 2, :], ACTF.Square).then_inc(l2_sq, 1)

            square(0)
            square(1)
            act.wait_ge(gates_mm, 1)
            act.activation(glo[:], pp[0:NG, 0, T:2 * T], ACTF.Copy).then_inc(gates_lo, 1)
            yield
            for g in range(HG):
                if g + 2 < HG:
                    square(g + 2)
                if g == 2:
                    act.wait_ge(gt_ready, 1)
                    act.activation(th[:], gt[:, :, 2 * HG:NG], ACTF.Tanh, scale=1.0 / CAP)
                    act.activation(beta[:], gt[:, :, HG:2 * HG], ACTF.Exp, scale=-1.0)
                    act.activation(rate[:], sm[:, S_ALOG:S_ALOG + HG], ACTF.Exp).then_inc(gt_act, 1)
                    act.wait_ge(sp_in, 1)
                    act.activation(spa[:], spa[:], ACTF.Exp).then_inc(act_step, 1)
                    act.wait_ge(act_step, 1)
                    act.activation(spa[:], spa[:], ACTF.Ln, bias=1.0).then_inc(sp_ln, 1)
                act.wait_ge(l2_mm, g + 1)
                act.activation(half(*sums[g]), pp[:, 2 + g % 2, :], ACTF.Ln, bias=eps[:]).then_inc(l2_ln, 1)
                if g % 2:
                    yield
            act.wait_ge(l2_ln, HG)
            for b in range(4):
                act.activation(tiles(sums[2 * b][0]), tiles(sums[2 * b][0]), ACTF.Exp, scale=-0.5).then_inc(l2_std, 1)
            act.wait_ge(gc_ready, 1)
            act.activation(egn[:], cum[:, :, 0:HG], ACTF.Exp).then_inc(eg_done, 1)
            yield
            yield
            for grp in range(2):
                yield from group_act(act, grp)
            act.wait_ge(o_done, 4)
            for p in range(pairs):
                act.activation(slot(*sums[p]), qkv[:, v_at + 2 * p:v_at + 2 * p + 2, :], ACTF.Square).then_inc(on_sq, 1)
            for p in range(pairs):
                act.wait_ge(on_mm, p + 1)
                act.activation(half(*sums[p]), pp[:, 2 + p % 2, :], ACTF.Ln, bias=eps[:], scale=1.0 / P).then_inc(on_ln, 1)
                if p % 2:
                    yield
            act.wait_ge(on_ln, pairs)
            for b in range(2):
                act.activation(tiles(sums[2 * b][0]), tiles(sums[2 * b][0]), ACTF.Exp, scale=-0.5).then_inc(on_std, 1)
            for m in range(HM):
                act.wait_ge(me_pre, m + 1)
                act.activation(mE[m % 2], mE[m % 2], ACTF.Exp, scale=-1.0).then_inc(me_exp, 1)
                act.activation(mX[:, m % 2], pp[:, 0, T:2 * T], ACTF.Exp).then_inc(mx_exp, 1)
                act.wait_ge(mv_mm, m + 1)
                act.activation(mV[m % 2], pp[:, 2, :].rearrange("p (a c) -> p a c", a=4), ACTF.Copy).then_inc(mvt_done, 1)
                yield
                for p in y_pairs(m):
                    act.wait_ge(on_pre, p + 1)
                    act.wait_ge(gz_done if p < 2 else mqk_mm, HM)
                    act.activation(hs[:, 2 * p:2 * p + 2, 0:T], qkv[:, v_at + 2 * p:v_at + 2 * p + 2, :], ACTF.Copy,
                                   scale=sm[:, S_GNW:S_GNW + 1]).then_inc(on_hi, 1)
                yield
            def mo_half_tanh(m):
                act.wait_ge(normed, mv_jobs + m + 1)
                mo = rest[:, mo_at + 2 * m:mo_at + 2 * m + 2, :]
                act.activation(mo, mo, ACTF.Tanh, scale=0.5).then_inc(mo_tanh, 1)

            act.wait_ge(mv_mm, HM)
            for m in range(HM - 1):
                mo_half_tanh(m)
            for m in range(HM):
                if m == HM - 1:
                    mo_half_tanh(m)
                act.wait_ge(my_pre, m + 1)
                act.activation(hs[:, HG + 2 * m:HG + 2 * m + 2, 0:T], mY[m % 2], ACTF.Copy).then_inc(my_hi, 1)
                if m:
                    yield

        def group_act(act, grp):
            act.wait_ge(rb_mm, grp + 1)
            for b in range(2):
                ins = act.activation(ER[:, 2 * b:2 * b + 2], pp[:, b, :].rearrange("p (h t) -> p h t", h=2)[:, :, C:T], ACTF.Exp)
            ins.then_inc(er_done, 1)
            yield
            act.wait_ge(rb_pre, grp + 1)
            act.activation(tiles(M), tiles(M), ACTF.Exp).then_inc(dec_exp, 1)
            if grp:
                for p in range(pairs):
                    ins = act.activation(gz_gate(p), rest[:, gz_at + 2 * p:gz_at + 2 * p + 2], ACTF.Tanh, scale=0.5)
                ins.then_inc(gz_tanh, 1)
            yield
            act.wait_ge(vt_mm, grp + 1)
            for h in range(4):
                act.activation(R[:, 0, h], bank(2, h), ACTF.Copy, scale=beta[:, 0, 4 * grp + h:4 * grp + h + 1])
                ins = act.activation(V1[:, h], bank(3, h), ACTF.Copy, scale=beta[:, 1, 4 * grp + h:4 * grp + h + 1])
            ins.then_inc(v_done, 1)
            yield
            yield
            act.wait_ge(y1_mm, grp + 1)
            for c in range(NCH):
                ins = act.activation(half(Y, c), pp[:, c, :], ACTF.Copy)
            ins.then_inc(y1_done, 1)
            yield
            for n in range(NL):
                act.wait_ge(z_mm, grp * NL + n + 1)
                for c in range(NCH):
                    ins = act.activation(half(Z, c), pp[:, 2 + c, :], ACTF.Copy)
                ins.then_inc(z_done, 1)
                yield
                yield
            act.wait_ge(vn_mm, 2 * grp + 1)
            act.activation(half(Z, 0), pp[:, 2, :], ACTF.Copy).then_inc(vn_done, 1)
            yield
            yield
            yield
            act.wait_ge(vn_mm, 2 * grp + 2)
            act.activation(half(Z, 1), pp[:, 1, :], ACTF.Copy).then_inc(vn_done, 1)
            yield
            yield

        def mixer_pool(pool):
            for grp in range(2):
                pool.wait_ge(dtr_done, grp + 1)
                pool.tensor_tensor(tiles(M), tiles(M), over(low, 8), ALU.mult).then_inc(m_low, 1)
                for n in range(NL):
                    if n == 0:
                        pool.wait_ge(x1_ready, grp + 1)
                    else:
                        pool.wait_ge(z_mm, grp * NL + n)
                    pool.tensor_tensor(tiles(L), tiles(M), over(level(n + 1), 2 * 4), ALU.mult).then_inc(l_ready, 1)
            pool.wait_ge(gz_done, pairs)
            for p in range(pairs):
                o = qkv[:, v_at + 2 * p:v_at + 2 * p + 2, :]
                pool.wait_ge(on_std, p // 2 + 1)
                pool.tensor_tensor(o, o, slot(*sums[p]), ALU.mult).then_inc(on_scaled, 1)
                pool.wait_ge(on_scaled, p + 1)
                pool.tensor_tensor(o, o, gz_gate(p), ALU.mult).then_inc(on_pre, 1)

        done = [0]

        def mixer_dve(dve):
            def step(ins):
                done[0] += 1
                ins.then_inc(dve_step, 1)
                dve.wait_ge(dve_step, done[0])

            dve.wait_ge(gates_lo, 1)
            step(dve.tensor_tensor(g24[:], pp[0:NG, 0, 0:T], glo[:], ALU.add))
            dve.tensor_tensor(g24[:], g24[:], rstd[0:NG, :], ALU.mult).then_inc(gates_sum, 1)
            yield
            dve.wait_ge(gates_t, 1)
            dve.tensor_tensor(gt[:], pp[:, 1, 0:64].rearrange("p (c n) -> p c n", c=2)[:, :, 0:NG],
                              over(sm[:, S_BIAS:S_BIAS + NG], NCH), ALU.add).then_inc(gt_ready, 1)
            yield
            dve.wait_ge(gt_act, 1)
            dve.tensor_scalar(ipre[:], th[:, :, 0:HM], CAP, None, ALU.mult)
            dve.wait_ge(gt_ready, 1)
            dve.tensor_copy(spi[:, :, 0:HG], gt[:, :, 0:HG])
            step(dve.tensor_scalar(spi[:, :, HG:HG + HM], th[:, :, HM:2 * HM], -CAP, None, ALU.mult))
            dve.scalar_tensor_tensor(spa[:], spi[:], -1.0, spi[:], ALU.mult, ALU.min).then_inc(sp_in, 1)
            step(dve.tensor_scalar(beta[:], beta[:], 1.0, None, ALU.add))
            step(dve.reciprocal(beta[:], beta[:]))
            yield
            dve.wait_ge(sp_ln, 1)
            step(dve.scalar_tensor_tensor(gl[:], spi[:], 0.0, spa[:], ALU.max, ALU.add))
            dve.scalar_tensor_tensor(gl[:, :, 0:HG], gl[:, :, 0:HG], -1.0, over(rate[:], NCH),
                                     ALU.mult, ALU.mult).then_inc(gl_ready, 1)
            yield
            yield
            dve.wait_ge(cum_mm, 1)
            dve.tensor_copy(cum[:].rearrange("p c n -> p (c n)"), pp[:, 0, 0:NCH * (HG + HM)]).then_inc(gc_ready, 1)
            dve.tensor_copy(gcrow[:], pp[0:HG, 1, 0:T])
            step(dve.tensor_copy(srow[:], pp[0:HM, 1, T:2 * T]))
            step(dve.tensor_tensor(arow[:], pp[0:HM, 0, T:2 * T], srow[:], ALU.add))
            step(dve.tensor_tensor_scan(mrow[:, 0, :], arow[:], arow[:], 0.0, ALU.max, ALU.max))
            dve.tensor_tensor(mrow[:, 1, :], srow[:], mrow[:, 0, :], ALU.subtract).then_inc(rows_ready, 1)
            for g in range(HG):
                if g == HG // 2:
                    yield
                dve.wait_ge(l2_std, g // 2 + 1)
                scale = float(P) ** -0.5 if g < HG // 2 else 1.0
                dve.scalar_tensor_tensor(qkv[:, 2 * g:2 * g + 2, :], qkv[:, 2 * g:2 * g + 2, :], scale, slot(*sums[g]),
                                         ALU.mult, ALU.mult).then_inc(l2_done, 1)
            dve.wait_ge(gc_ready, 1)
            dve.tensor_tensor(acol[:], ipre[:], cum[:, :, HG:HG + HM], ALU.add)
            dve.wait_ge(eg_done, 1)
            step(dve.scalar_tensor_tensor(egn[:], egn[:], -1.0, beta[:], ALU.mult, ALU.mult))
            yield
            for grp in range(2):
                yield from group_dve(dve, grp, step)
            yield
            yield
            def weights_exponent(m):
                dve.wait_ge(mb_mm, m + 1)
                e = mE[m % 2]
                dve.tensor_scalar(e[:, 0:T], pp[:, 0, 0:T], acol[:, 0, m:m + 1], 0.0, ALU.subtract, ALU.max)
                dve.tensor_scalar(e[:, T:3 * C], pp[:, 0, C:T], acol[:, 1, m:m + 1], 0.0, ALU.subtract,
                                  ALU.max).then_inc(me_pre, 1)

            weights_exponent(0)
            for m in range(HM):
                e = mE[m % 2]
                diag = e.rearrange("p (a c) -> p a c", a=3)[:, 0:3:2]
                dve.wait_ge(me_exp, m + 1)
                step(dve.tensor_tensor(diag, diag, over(tri, 2), ALU.mult))
                dve.wait_ge(mqk_mm, m + 1)
                dve.scalar_tensor_tensor(mP[m % 2], pp[:, 1, 0:3 * C], float(P) ** -0.5, e, ALU.mult, ALU.mult).then_inc(p_done, 1)
                yield
                dve.wait_ge(on_pre, m + 1)
                dve.wait_ge(mx_exp, m + 1)
                dve.wait_ge(num_mm, m + 1)
                dn = mDn[:, m % 2]
                step(dve.tensor_tensor(dn, pp[:, 1, 0:T], mX[:, m % 2], ALU.max))
                dve.scalar_tensor_tensor(dn, pp[:, 1, 0:T], -1.0, dn, ALU.mult, ALU.max).then_inc(den_read, 1)
                dve.wait_ge(den_read, m + 1)
                step(dve.reciprocal(dn, dn))
                dve.scalar_tensor_tensor(qkv[:, 2 * m:2 * m + 2, :], pp[:, 3, :].rearrange("p (e t) -> p e t", e=2), 0.5,
                                         over(dn, 2), ALU.mult, ALU.mult).then_inc(mh_done, 1)
                if m + 1 < HM:
                    weights_exponent(m + 1)
                for p in y_pairs(m):
                    dve.wait_ge(on_hi, p + 1)
                    dve.scalar_tensor_tensor(hs[:, 2 * p:2 * p + 2, T:2 * T], qkv[:, v_at + 2 * p:v_at + 2 * p + 2, :],
                                             sm[:, S_GNW:S_GNW + 1], hs[:, 2 * p:2 * p + 2, 0:T].bitcast(F32),
                                             ALU.mult, ALU.subtract).then_inc(y_split, 1)
                yield
            def gate_mlstm(m):
                dve.wait_ge(mo_tanh, m + 1)
                dve.wait_ge(mh_done, m + 1)
                if m >= 2:
                    dve.wait_ge(y_split, pairs + m - 1)
                dve.scalar_tensor_tensor(mY[m % 2], rest[:, mo_at + 2 * m:mo_at + 2 * m + 2, :], 1.0,
                                         qkv[:, 2 * m:2 * m + 2, :], ALU.add, ALU.mult).then_inc(my_pre, 1)

            gate_mlstm(0)
            for m in range(HM):
                if m < 2:
                    gate_mlstm(m + 1)
                if m == HM - 1:
                    gate_mlstm(m)
                dve.wait_ge(my_hi, m + 1)
                y = slice(HG + 2 * m, HG + 2 * m + 2)
                dve.tensor_tensor(hs[:, y, T:2 * T], mY[m % 2], hs[:, y, 0:T].bitcast(F32), ALU.subtract).then_inc(y_split, 1)
                if m:
                    yield

        def group_dve(dve, grp, step):
            h0 = 4 * grp
            dve.wait_ge(er_done, grp + 1)
            for c in range(NCH):
                rows = pp[:, 0:2, :].rearrange("p b (h t) -> p (b h) t", h=2)[:, :, c * C:(c + 1) * C]
                cols = cum[:, c, h0:h0 + 4].rearrange("p (h a) -> p h a", a=1).to_broadcast([P, 4, C])
                ins = dve.tensor_tensor(M[:, c], rows, cols, ALU.subtract)
            ins.then_inc(rb_diff, 1)
            dve.wait_ge(rb_diff, grp + 1)
            dve.scalar_tensor_tensor(tiles(M), tiles(M), -1.0, tiles(M), ALU.mult, ALU.min).then_inc(rb_pre, 1)
            yield
            dve.wait_ge(dec_exp, grp + 1)
            dve.tensor_tensor(tiles(DTr), tiles(M), over(tri, 8), ALU.mult).then_inc(dtr_done, 1)
            dve.wait_ge(dtr_done, grp + 1)
            step(dve.tensor_copy(dcol[:], DTr[:, 0, :, C - 1]))
            dve.wait_ge(qk_mm, grp + 1)
            for c in range(NCH):
                ins = dve.tensor_tensor(half(DTr, c), pp[:, 2 + c, :], half(DTr, c), ALU.mult)
            ins.then_inc(at_done, 1)
            yield
            dve.wait_ge(kk_mm, grp + 1)
            dve.wait_ge(m_low, grp + 1)
            for c in range(NCH):
                for h in range(4):
                    ins = dve.scalar_tensor_tensor(M[:, c, h], bank(c, h), beta[:, c, h0 + h:h0 + h + 1], M[:, c, h],
                                                   ALU.mult, ALU.mult)
            ins.then_inc(m_done, 1)
            dve.wait_ge(m_done, grp + 1)
            step(dve.tensor_tensor(tiles(L), tiles(M), over(level(0), 8), ALU.mult))
            dve.tensor_tensor(tiles(X), over(ident, 8), tiles(L), ALU.subtract).then_inc(x1_ready, 1)
            yield
            dve.wait_ge(kt_mm, grp + 1)
            for h in range(4):
                ins = dve.tensor_scalar(KD[:, h], bank(0, h), dcol[:, h:h + 1], None, ALU.mult)
            ins.then_inc(kd_done, 1)
            yield
            yield
            for n in range(NL):
                if grp and n < 4:
                    dve.wait_ge(gz_tanh, 1)
                    dve.scalar_tensor_tensor(gz_gate(n), gz_gate(n), 1.0, rest[:, gz_at + 2 * n:gz_at + 2 * n + 2, :],
                                             ALU.add, ALU.mult).then_inc(gz_done, 1)
                yield
                dve.wait_ge(yz_mm, grp * NL + n + 1)
                if n == 0:
                    dve.wait_ge(y1_done, grp + 1)
                for c in range(NCH):
                    y = every_second(half(Y, c), n, 1)
                    ins = dve.tensor_tensor(y, y, every_second(pp[:, c, :], n, 1), ALU.subtract)
                ins.then_inc(y_done, 1)
                if n < NL - 1:
                    dve.wait_ge(xz_mm, grp * (NL - 1) + n + 1)
                    for c in range(NCH):
                        x_even = every_second(half(X, c), n, 0)
                        ins = dve.tensor_tensor(x_even, x_even, every_second(pp[:, 2 + c, :], n, 0), ALU.subtract)
                    ins.then_inc(x_done, 1)
                yield
            dve.wait_ge(z_mm, (grp + 1) * NL)
            dve.tensor_tensor(L[:, 1], qkv[:, q_at + h0:q_at + h0 + 4, C:T], ER[:], ALU.mult).then_inc(qd_done, 1)
            yield
            dve.wait_ge(s1_mm, grp + 1)
            dve.tensor_copy(half(L, 0), pp[:, 3, :]).then_inc(s1_done, 1)
            yield
            dve.wait_ge(ks_mm, grp + 1)
            for h in range(4):
                ins = dve.scalar_tensor_tensor(R[:, 1, h], bank(0, h), egn[:, 1, h0 + h:h0 + h + 1], V1[:, h],
                                               ALU.mult, ALU.add)
            ins.then_inc(r1_done, 1)
            dve.wait_ge(o_mm, 2 * grp + 1)
            copy_out(dve, h0, 0)
            yield
            yield
            dve.wait_ge(o_mm, 2 * grp + 2)
            copy_out(dve, h0, 1)
            yield

        def copy_out(dve, h0, c):
            o = qkv[:, v_at + h0:v_at + h0 + 4, c * C:(c + 1) * C]
            dve.tensor_copy(o, pp[:, 2 + c, :].rearrange("p (h c) -> p h c", h=4)).then_inc(o_done, 1)

        block = ctx.enter_context(nc.Block())

        @block.sync
        def _(sp):
            x_dram = x.rearrange("(k p) t -> p k t", p=P)
            sp.dma_start(sm[:], small).then_inc(small_in, 16)
            for s in range(STAGES):
                sp.dma_start(res[:, 4 * s:4 * s + 4, :], x_dram[:, 4 * s:4 * s + 4, :]).then_inc(x_in[s], 16)
                sp.dma_start(st[:, s].rearrange("p k n -> p (k n)"), stream[s]).then_inc(staged[s], 16)
            with sp.Fori(1, UNITS // STAGES) as i:
                for s in range(STAGES):
                    sp.wait_ge(split, i * STAGES + (s + 1))
                    sp.dma_start(st[:, s].rearrange("p k n -> p (k n)"),
                                 stream[bass.ds(i * STAGES + s, 1)].rearrange("u p n -> (u p) n")).then_inc(staged[s], 16)
            for q in range(DT_ // 4):
                sp.wait_ge(t_ready, q + 1)
                sp.dma_start(out[q * 4 * P:(q + 1) * 4 * P, :].rearrange("(k p) t -> p k t", p=P),
                             fin[:, 4 * q:4 * q + 4, :]).then_inc(out_done[q % 2], 16)
            for b in range(2):
                sp.wait_ge(out_done[b], 16 * (DT_ // 8))

        @block.gpsimd
        def _(pool):
            pool.wait_ge(unit_done, SLOTS + 4)
            pool.dma_start(kc[:], consts).then_inc(consts_in, 16)
            pool.wait_ge(unit_done, SLOTS + U_FFN)
            pool.dma_start(wgf[:].rearrange("p k n -> p (k n)"), wg).then_inc(wg_in, 16)
            mixer_pool(pool)

        @block.tensor
        def _(pe):
            def job(i, name, jj, rhs, before_unit, side, norm):
                u0, j0, per, n_units, _ = plan[name]
                pe.wait_ge(bank_free, i * per + (j0 + jj + 1))
                for u in range(n_units):
                    g = jj * n_units + u
                    s = g % SLOTS
                    pe.wait_ge(split, i * (per * n_units) + (STAGES + u0 + g + 1))
                    before_unit(jj, u)
                    for n in range(2):
                        for k in range(UK):
                            kt, last = u * UK + k, u == n_units - 1 and k == UK - 1
                            cols = slice(n * P, (n + 1) * P)
                            pe.matmul(pg[:, jj % 2, n, :], whi[:, s, k, cols], rhs[:, kt, :],
                                      start=u == 0 and k == 0, stop=False, skip_group_check=True)
                            mm = pe.matmul(pg[:, jj % 2, n, 0:T], wlo[:, s, k, cols], rhs[:, kt, 0:T],
                                           start=False, stop=last, skip_group_check=True)
                    mm.then_inc(unit_done, 1)
                    next(side, None)
                    if norm is not None and isinstance(i, int) and (i, g) == (0, n_units + 1 if norm == 0 else n_units - 1):
                        total_squares(norm)

            def phase(name, rhs, before_unit, side=iter(()), norm=None):
                for i in rounds_of(pe, name):
                    for jj in range(plan[name][2]):
                        job(i, name, jj, rhs, before_unit, side, norm)

            def after_norm(n):
                def before(jj, u):
                    if jj == 0:
                        pe.wait_ge(x_ready, n * NJD + 2 * (u + 1))
                return before

            def after_blocks(first):
                def before(jj, u):
                    if jj == 0:
                        pe.wait_ge(h_split, 1 + first + UK // 2 * (u + 1))
                return before

            def after_mixer(jj, u):
                if jj == 0:
                    pe.wait_ge(y_split, 2 * (u + 1))

            def total_squares(n):
                pe.wait_ge(ssq_part, (n + 1) * (NJD + 1))
                pe.matmul(pp[:, 0, 0:T], ones_t[:], ssq[:, 0, :], start=True, stop=False)
                pe.matmul(pp[:, 0, 0:T], ones_t[:], ssq[:, 1, :], start=False, stop=True).then_inc(ssq_mm, 1)

            def ffn(n, norm, block0):
                phase(f"ffn{n}_up_a", xs, after_norm(norm), norm=norm)
                phase(f"ffn{n}_down_a", hs, after_blocks(block0))
                phase(f"ffn{n}_up_b", xs, after_norm(norm))
                phase(f"ffn{n}_down_b", hs, after_blocks(block0 + BLK_A))

            pe.sem_inc(unit_done, SLOTS)
            pe.wait_ge(fills, 2)
            ffn(1, 0, 0)
            phase("in_qkv", xs, after_norm(1), norm=1)
            side = mixer_pe(pe)
            phase("in_rest", xs, after_norm(1), side)
            for _ in side:
                pass
            phase("out", hs, after_mixer)
            ffn(2, 2, BLK_A + BLK_B)
            total_squares(3)

        @block.scalar
        def _(act):
            def split_unit(i, per_round, g):
                if isinstance(i, int) and i * per_round + g >= UNITS:
                    return
                s = g % SLOTS
                act.wait_ge(staged[s], i * (16 * per_round // STAGES) + 16 * (g // STAGES + 1))
                act.wait_ge(unit_done, i * per_round + (g + 1))
                act.activation(whi[:, s], st[:, s], ACTF.Copy).then_inc(hi_ready, 1)

            def phase(name, scale, finish, side=iter(()), beside_norm=None):
                u0, j0, per, n_units, rounds = plan[name]
                late = 1 if name == "in_rest" else 2
                for i in rounds_of(act, name):
                    for jj in range(per):
                        first = u0 + jj * n_units + SLOTS
                        for u in range(n_units - late):
                            split_unit(i, per * n_units, first + u)
                            next(side, None)
                        act.wait_ge(unit_done, i * (per * n_units) + (SLOTS + u0 + (jj + 1) * n_units))
                        act.activation(tmp[:, jj % 2], pg[:, jj % 2, :, T:2 * T], ACTF.Copy, scale=scale).then_inc(lo_copied, 1)
                        for u in range(n_units - late, n_units):
                            split_unit(i, per * n_units, first + u)
                            next(side, None)
                        if beside_norm and isinstance(i, int) and i == jj == 0:
                            beside_norm()
                        if finish:
                            finish(i, jj)

            def block_finish(name, block0):
                def finish(i, jj):
                    if jj == 0:
                        act.wait_ge(normed, i * 2 + (normed0[name] + 1))
                        act.activation(sg[:], gsum[:], ACTF.Tanh, scale=0.5).then_inc(gate_tanh, 1)
                    else:
                        act.wait_ge(h_ready, i + (block0 + 1))
                        act.activation(hs[:, bass.ds(i * 2, 2), 0:T], hp[:], ACTF.Copy).then_inc(h_hi, 1)
                return finish

            def residual_finish(name, r0, q0, n):
                per = plan[name][2]
                def finish(i, jj):
                    act.wait_ge(res_done, i * per + (r0 + jj + 1))
                    if n < 3:
                        for e in range(2):
                            round_x(n, i * (2 * per) + (2 * jj + e))
                    act.activation(sq[:], res[:, bass.ds(i * (2 * per) + 2 * jj, 2), :],
                                   ACTF.Square).then_inc(sq_done, 1)
                    if n == 3:
                        for tile in range(i * 2 * per + 2 * jj, i * 2 * per + 2 * jj + 2):
                            act.activation(fin[:, tile], res[:, tile, :], ACTF.Copy, scale=w_cols(3, tile)).then_inc(gained, 1)
                return finish

            def round_x(n, tile):
                t = bass.ds(tile, 1)
                act.activation(xs[:, t, 0:T], res[:, t, :], ACTF.Copy,
                               scale=w_cols(n, tile)).then_inc(x_hi, 1)

            def norm(n):
                act.wait_ge(ssq_mm, n + 1)
                act.activation(rstd[:], pp[:, 0, 0:T], ACTF.Ln, bias=eps[:], scale=1.0 / D).then_inc(ln_done, 1)
                act.wait_ge(ln_done, n + 1)
                act.activation(rstd[:], rstd[:], ACTF.Exp, scale=-0.5).then_inc(rstd_done, 1)

            def ffn(n, block0, jobs0, squares0, norm_before, norm_after, side=iter(())):
                phase(f"ffn{n}_up_a", 1.0, block_finish(f"ffn{n}_up_a", block0), side, lambda: norm(norm_before))
                phase(f"ffn{n}_down_a", 0.5, None)
                phase(f"ffn{n}_up_b", 1.0, block_finish(f"ffn{n}_up_b", block0 + BLK_A))
                phase(f"ffn{n}_down_b", 0.5, residual_finish(f"ffn{n}_down_b", jobs0 + NJD, squares0, norm_after))

            act.wait_ge(fills, 2)
            act.activation(warm[:], eps[:], ACTF.Copy)
            act.wait_ge(small_in, 16)
            for q in range(4):
                act.wait_ge(x_in[q], 16)
                for e in range(4):
                    round_x(0, 4 * q + e)
                split_unit(0, 0, q)

            def square_x():
                for q in range(4):
                    act.activation(xq[:, 4 * q:4 * q + 4, :], res[:, 4 * q:4 * q + 4, :], ACTF.Square).then_inc(x_sq, 1)
                    if q:
                        yield

            side = square_x()
            next(side)
            ffn(1, 0, 0, 0, 0, 1, side)
            act.wait_ge(fills, 5)

            def qkv_finish(i, jj):
                act.wait_ge(normed, i * 2 + (normed0["in_qkv"] + jj + 1))
                for n in range(2):
                    tap = sm[:, bass.ds(i * (4 * CW) + (S_CONV + (2 * jj + n) * CW + CW - 1), 1)]
                    ins = act.activation(cv[:, n], raw[:, n, CW - 1:CW - 1 + T], ACTF.Copy, scale=tap)
                ins.then_inc(tap0, 1)
                act.wait_ge(conv_step, i * (2 * (CW - 1)) + (jj + 1) * (CW - 1))
                act.activation(cth[:], cv[:], ACTF.Tanh).then_inc(conv_tanh, 1)
                if isinstance(i, int) and jj == 1:
                    act.wait_ge(wg_in, 16)
                    act.activation(wgh[:], wgf[:], ACTF.Copy).then_inc(wg_hi, 1)

            phase("in_qkv", 1.0, qkv_finish, beside_norm=lambda: norm(1))
            side = mixer_act(act)
            phase("in_rest", 1.0, None, side)
            for _ in side:
                pass
            phase("out", 1.0, residual_finish("out", 2 * NJD, NJD, 2))
            ffn(2, BLK_A + BLK_B, 3 * NJD, 2 * NJD, 2, 3)
            norm(3)

        @block.vector
        def _(dve):
            def split_unit(i, per_round, g):
                if isinstance(i, int) and i * per_round + g >= UNITS:
                    return
                s = g % SLOTS
                dve.wait_ge(hi_ready, i * per_round + (g + 1))
                dve.tensor_tensor(wlo[:, s], st[:, s], whi[:, s].bitcast(F32), ALU.subtract).then_inc(split, 1)

            def evacuate(i, jj, name, add):
                j0, per = plan[name][1:3]
                dve.wait_ge(lo_copied, i * per + (j0 + jj + 1))
                ins, total = add(i, jj, pg[:, jj % 2, :, 0:T], tmp[:, jj % 2])
                ins.then_inc(bank_free, 1)
                return total

            def scale(i, jj, name, total):
                j0, per = plan[name][1:3]
                if name in normed0:
                    if isinstance(i, int) and i == jj == 0 and name in norm_of:
                        dve.wait_ge(rstd_done, norm_of[name] + 1)
                    dve.wait_ge(bank_free, i * per + (2 + j0 + jj + 1))
                    dve.tensor_tensor(total, total, over(rstd[:], 2), ALU.mult).then_inc(normed, 1)

            def phase(name, add, finish, side=iter(())):
                u0, j0, per, n_units, rounds = plan[name]
                late = 1 if name == "in_rest" else 2
                for i in rounds_of(dve, name):
                    for jj in range(per):
                        first = u0 + jj * n_units + SLOTS
                        for u in range(n_units - late):
                            split_unit(i, per * n_units, first + u)
                            next(side, None)
                        total = evacuate(i, jj, name, add)
                        wait_for_norm = name in norm_of and isinstance(i, int) and i == jj == 0
                        if not wait_for_norm:
                            scale(i, jj, name, total)
                        for u in range(n_units - late, n_units):
                            split_unit(i, per * n_units, first + u)
                            next(side, None)
                        if wait_for_norm:
                            scale(i, jj, name, total)
                        if finish:
                            finish(i, jj)

            def add_gate_or_up(i, jj, hi, lo):
                total = (gsum if jj == 0 else usum)[:]
                return dve.tensor_tensor(total, hi, lo, ALU.add), total

            def block_finish(name, block0):
                def finish(i, jj):
                    if jj == 0:
                        dve.wait_ge(gate_tanh, i + (block0 + 1))
                        dve.scalar_tensor_tensor(sg[:], sg[:], 1.0, gsum[:], ALU.add, ALU.mult).then_inc(gate_act, 1)
                    else:
                        dve.wait_ge(gate_act, i + (block0 + 1))
                        dve.wait_ge(h_split, i + (block0 + 1))
                        dve.wait_ge(normed, i * 2 + (normed0[name] + 2))
                        dve.scalar_tensor_tensor(hp[:], sg[:], 0.5, usum[:], ALU.mult, ALU.mult).then_inc(h_ready, 1)
                        dve.wait_ge(h_hi, i + (block0 + 1))
                        t = bass.ds(i * 2, 2)
                        dve.tensor_tensor(hs[:, t, T:2 * T], hp[:], hs[:, t, 0:T].bitcast(F32),
                                          ALU.subtract).then_inc(h_split, 1)
                return finish

            def add_scaled(scale):
                return lambda i, jj, hi, lo: (dve.scalar_tensor_tensor(gsum[:], hi, scale, lo, ALU.mult, ALU.add), gsum[:])

            def clear_squares(n):
                dve.memset(ssq[:], 0.0).then_inc(ssq_part, 1)
                dve.wait_ge(ssq_part, n * (NJD + 1) + 1)

            def residual_finish(name, r0, q0, n):
                j0, per = plan[name][1:3]
                def finish(i, jj):
                    dve.wait_ge(bank_free, i * per + (2 + j0 + jj + 1))
                    t = bass.ds(i * 2 * per + 2 * jj, 2)
                    dve.tensor_tensor(res[:, t, :], res[:, t, :], gsum[:], ALU.add).then_inc(res_done, 1)
                    dve.wait_ge(res_done, i * per + (r0 + jj + 1))
                    if n is not None:
                        if n < 3:
                            for e in range(2):
                                dve.wait_ge(x_hi, i * (2 * per) + (n * DT_ + 2 * jj + e + 1))
                                ins = remainder(n, i * (2 * per) + (2 * jj + e))
                            ins.then_inc(x_ready, 1)
                        dve.wait_ge(sq_done, i * per + (q0 + jj + 1))
                        dve.tensor_tensor(ssq[:], ssq[:], sq[:], ALU.add).then_inc(ssq_part, 1)
                        dve.wait_ge(ssq_part, i * per + (n * (NJD + 1) + 1 + jj + 1))
                return finish

            def remainder(n, tile):
                t = bass.ds(tile, 1)
                return dve.scalar_tensor_tensor(xs[:, t, T:2 * T], res[:, t, :], w_cols(n, tile), xs[:, t, 0:T].bitcast(F32),
                                                ALU.mult, ALU.subtract)

            def ffn(n, block0, jobs0, squares0, norm_after, side=iter(())):
                phase(f"ffn{n}_up_a", add_gate_or_up, block_finish(f"ffn{n}_up_a", block0), side)
                phase(f"ffn{n}_down_a", add_scaled(0.5), residual_finish(f"ffn{n}_down_a", jobs0, None, None))
                phase(f"ffn{n}_up_b", add_gate_or_up, block_finish(f"ffn{n}_up_b", block0 + BLK_A))
                clear_squares(norm_after)
                phase(f"ffn{n}_down_b", add_scaled(0.5),
                      residual_finish(f"ffn{n}_down_b", jobs0 + NJD, squares0, norm_after))

            dve.memset(ones_t[:], 1.0).then_inc(fills, 1)
            dve.memset(eps[:], EPS).then_inc(fills, 1)
            dve.sem_inc(split, STAGES)
            dve.sem_inc(bank_free, 2)
            dve.sem_inc(h_split, 1)
            dve.wait_ge(small_in, 16)
            for q in range(4):
                for e in range(4):
                    dve.wait_ge(x_hi, 4 * q + e + 1)
                    ins = remainder(0, 4 * q + e)
                    if e % 2:
                        ins.then_inc(x_ready, 1)
                split_unit(0, 0, q)

            def sum_x_squares():
                dve.wait_ge(x_sq, 2)
                dve.tensor_tensor(xq[:, 0:4], xq[:, 0:4], xq[:, 4:8], ALU.add).then_inc(x_sq_sum, 1)
                yield
                for q in range(2, 4):
                    dve.wait_ge(x_sq, q + 1)
                    dve.wait_ge(x_sq_sum, q - 1)
                    dve.tensor_tensor(xq[:, 0:4], xq[:, 0:4], xq[:, 4 * q:4 * q + 4], ALU.add).then_inc(x_sq_sum, 1)
                    if q == 2:
                        yield
                dve.wait_ge(x_sq_sum, 3)
                dve.tensor_tensor(ssq[:], xq[:, 0:2], xq[:, 2:4], ALU.add).then_inc(ssq_part, NJD + 1)
                yield

            side = sum_x_squares()
            next(side)
            ffn(1, 0, 0, 0, 1, side)

            dve.tensor_scalar(sm[:, S_CONV:S_GNW + 1], sm[:, S_CONV:S_GNW + 1], 0.5, None, ALU.mult).then_inc(fills, 1)
            dve.memset(raw[:, 0, 0:CW - 1], 0.0).then_inc(fills, 1)
            dve.memset(raw[:, 1, 0:CW - 1], 0.0).then_inc(fills, 1)
            dve.wait_ge(fills, 5)

            def add_qkv(i, jj, hi, lo):
                total = raw[:, :, CW - 1:CW - 1 + T]
                return dve.tensor_tensor(total, hi, lo, ALU.add), total

            def qkv_finish(i, jj):
                job = i * 2 + (jj + 1)
                dve.wait_ge(tap0, job)
                for w in range(1, CW):
                    for n in range(2):
                        tap = sm[:, bass.ds(i * (4 * CW) + (S_CONV + (2 * jj + n) * CW + CW - 1 - w), 1)]
                        ins = dve.scalar_tensor_tensor(cv[:, n], raw[:, n, CW - 1 - w:CW - 1 - w + T], tap, cv[:, n],
                                                       ALU.mult, ALU.add)
                    ins.then_inc(conv_step, 1)
                    if w < CW - 1:
                        dve.wait_ge(conv_step, i * (2 * (CW - 1)) + (jj * (CW - 1) + w))
                dve.wait_ge(conv_tanh, job)
                dve.scalar_tensor_tensor(qkv[:, bass.ds(i * 4 + 2 * jj, 2), :], cth[:], 1.0, cv[:],
                                         ALU.add, ALU.mult).then_inc(qkv_done, 1)
                if isinstance(i, int) and jj == 1:
                    dve.wait_ge(wg_hi, 1)
                    dve.tensor_tensor(wgl[:], wgf[:], wgh[:].bitcast(F32), ALU.subtract).then_inc(wg_split, 1)

            def add_rest(i, jj, hi, lo):
                total = rest[:, bass.ds(i * 4 + 2 * jj, 2), :]
                return dve.tensor_tensor(total, hi, lo, ALU.add), total

            phase("in_qkv", add_qkv, qkv_finish)
            side = mixer_dve(dve)
            phase("in_rest", add_rest, None, side)
            for _ in side:
                pass
            clear_squares(2)
            phase("out", add_scaled(1.0), residual_finish("out", 2 * NJD, NJD, 2))
            ffn(2, BLK_A + BLK_B, 3 * NJD, 2 * NJD, 3)
            dve.wait_ge(rstd_done, 4)
            for q in range(DT_ // 4):
                dve.wait_ge(gained, 4 * (q + 1))
                y = fin[:, 4 * q:4 * q + 4, :]
                dve.tensor_tensor(y, y, over(rstd[:], 4), ALU.mult).then_inc(t_ready, 1)


def lay_out(inputs):
    a = {k: np.asarray(v) for k, v in inputs.items()}

    def units(w, rows, cols):
        w = w[rows, cols]
        return w.reshape(w.shape[0] // (UK * P), UK, P, w.shape[1] // UN, UN).transpose(3, 0, 2, 1, 4)

    def flat(u):
        return u.reshape(-1, P, UK * UN)

    def ffn(n):
        gate, up, down = (a[f"ffn{n}_w_{x}"][0] for x in ("gate", "up", "down"))
        parts = []
        for first, blocks in ((0, BLK_A), (BLK_A, BLK_B)):
            f = slice(first * UN, (first + blocks) * UN)
            every = slice(None)
            parts.append(flat(np.stack([units(gate, every, f), units(up, every, f)], axis=1)))
            parts.append(flat(units(down, f, every)))
        return parts

    w_in = a["w_in"][0]
    gqkvz, gab = HG * 4 * P, 2 * HG
    mqkvo = (2 * HM + 2 * 2 * HM) * P
    every = slice(None)
    stream = np.concatenate(
        ffn(1) + [flat(units(w_in, every, slice(0, gqkvz))), flat(units(w_in, every, slice(gqkvz + gab, gqkvz + gab + mqkvo))),
                  flat(units(a["w_out"][0], every, every))] + ffn(2))
    wg = np.concatenate([w_in[:, gqkvz:gqkvz + gab], w_in[:, gqkvz + gab + mqkvo:]], axis=1)
    wg = wg.reshape(DT_, P, NG).transpose(1, 0, 2).reshape(P, DT_ * NG)

    def columns(v):
        return v.reshape(-1, P).T

    def on_all(row):
        return np.broadcast_to(row, (P, row.shape[-1]))

    conv = a["conv_w"][0].reshape(CW, NQKV, P).transpose(2, 1, 0).reshape(P, NQKV * CW)
    bias = np.concatenate([a["gdn_dt_bias"][0], np.zeros(HG, np.float32), a["ml_i_bias"][0], a["ml_f_bias"][0]])
    small = np.concatenate([columns(a["ffn1_norm_w"]), columns(a["mix_norm_w"]), columns(a["ffn2_norm_w"]),
                            columns(a["final_norm_w"]), conv, columns(a["gdn_norm_w"]), on_all(bias),
                            on_all(a["gdn_a_log"][0])], axis=1)
    return {"stream": stream, "x": a["x"][0].T, "wg": wg, "small": small, "consts": constants()}


def kernel(**inputs):
    import concourse.bacc as bacc
    from concourse.bass_utils import run_bass_kernel_spmd as run

    nc = bacc.Bacc("TRN2", target_bir_lowering=False, num_devices=1)
    arrays, args = {}, []
    for name, a in lay_out(inputs).items():
        a = np.ascontiguousarray(a)
        arrays[f"in_{name}_dram"] = a
        args.append(nc.dram_tensor(f"in_{name}_dram", a.shape, mybir.dt.from_np(a.dtype), kind="ExternalInput").ap())
    args.append(nc.dram_tensor("out_0_dram", (D, T), F32, kind="ExternalOutput").ap())
    build(nc, *args)
    r = run(nc, [arrays], core_ids=[0])
    return np.ascontiguousarray(r.results[0]["out_0_dram"].T).reshape(1, T, D)
```
